# Optimizing a Trainium2 kernel written in Bass

```python
import jax, jax.numpy as jnp
from jax import lax
import numpy as np
import math
import jax
import jax.numpy as jnp

D_MODEL = 1024
BATCH = 1
SEQ = 256
DEPTH = 2

N_A = DEPTH // 2
N_B = DEPTH - N_A
N_DENSE = (DEPTH + 1) // 2
N_MOE = DEPTH // 2

GLA_HEADS = 4
GLA_DK = D_MODEL // 2 // GLA_HEADS
GLA_DV = D_MODEL // GLA_HEADS
GLA_QK = GLA_HEADS * GLA_DK
GLA_V = GLA_HEADS * GLA_DV
GLA_GATE_RANK = 16
GLA_GATE_NORM = 16.0
GLA_CHUNK = 64
GLA_IN = 2 * GLA_QK + GLA_V + GLA_GATE_RANK + GLA_V

SB_HEADS = 8
SB_HEAD_DIM = D_MODEL // SB_HEADS
SB_BLOCK = 128

FFN_DIM = 2816
N_EXPERTS = 8
TOP_K = 2
EXPERT_DIM = 3584

RMS_EPS = 1e-6


def rms_norm(x, g):
    xf = x.astype(jnp.float32)
    y = xf * lax.rsqrt(jnp.mean(xf * xf, axis=-1, keepdims=True) + RMS_EPS)
    return (y * g.astype(jnp.float32)).astype(x.dtype)

def swiglu(h, w_gate, w_up, w_down):
    return (jax.nn.silu(h @ w_gate) * (h @ w_up)) @ w_down

def gla_mixer(h, w_in, w_gate_up, b_gate, g_head, w_out):
    B, S, _ = h.shape
    H, dk, dv, C = GLA_HEADS, GLA_DK, GLA_DV, GLA_CHUNK
    nc = S // C
    proj = h @ w_in
    q, k, v, g_lr, r = jnp.split(
        proj, [GLA_QK, 2 * GLA_QK, 2 * GLA_QK + GLA_V, 2 * GLA_QK + GLA_V + GLA_GATE_RANK], axis=-1)
    log_a = jax.nn.log_sigmoid((g_lr @ w_gate_up + b_gate).astype(jnp.float32)) / GLA_GATE_NORM

    def to_chunks(t, d):
        return t.reshape(B, nc, C, H, d).transpose(1, 0, 3, 2, 4).astype(jnp.float32)

    qc = to_chunks(q, dk) * (dk ** -0.5)
    kc = to_chunks(k, dk)
    vc = to_chunks(v, dv)
    gc = to_chunks(log_a, dk)
    b = jnp.cumsum(gc, axis=3)
    b_end = b[:, :, :, -1:, :]
    q_dec = qc * jnp.exp(b)
    k_inv = kc * jnp.exp(-b)
    k_end = kc * jnp.exp(b_end - b)
    decay_end = jnp.exp(b_end[:, :, :, 0, :])

    tri = jnp.tril(jnp.ones((C, C), dtype=bool))
    attn = jnp.where(tri, jnp.einsum('nbhid,nbhjd->nbhij', q_dec, k_inv), 0.0)
    o_intra = jnp.einsum('nbhij,nbhjv->nbhiv', attn, vc)

    def step(state, inp):
        q_n, k_n, v_n, dec_n = inp
        o_n = jnp.einsum('bhid,bhdv->bhiv', q_n, state)
        state = dec_n[..., None] * state + jnp.einsum('bhid,bhiv->bhdv', k_n, v_n)
        return state, o_n

    state0 = jnp.zeros((B, H, dk, dv), dtype=jnp.float32)
    _, o_inter = lax.scan(step, state0, (q_dec, k_end, vc, decay_end))
    o = (o_inter + o_intra).transpose(1, 0, 3, 2, 4).reshape(B, S, H, dv)
    o = rms_norm(o, g_head).reshape(B, S, GLA_V)
    o = (o * jax.nn.silu(r.astype(jnp.float32))).astype(h.dtype)
    return o @ w_out

def stick_breaking_mixer(h, k, v, w_q, w_out):
    B, S, _ = h.shape
    H, hd = SB_HEADS, SB_HEAD_DIM
    q = (h @ w_q).reshape(B, S, H, hd).transpose(0, 2, 1, 3)
    scale = hd ** -0.5
    outs = []
    for blk in range(S // SB_BLOCK):
        t0 = blk * SB_BLOCK
        t1 = t0 + SB_BLOCK
        qb = q[:, :, t0:t1]
        kb = k[:, :, :t1]
        vb = v[:, :, :t1]
        z = jnp.einsum('bhtd,bhsd->bhts', qb, kb).astype(jnp.float32) * scale
        t_idx = t0 + jnp.arange(SB_BLOCK)[:, None]
        s_idx = jnp.arange(t1)[None, :]
        causal = s_idx < t_idx
        log_beta = jax.nn.log_sigmoid(z)
        log_keep = jnp.where(causal, jax.nn.log_sigmoid(-z), 0.0)
        log_stay = lax.cumsum(log_keep, axis=3, reverse=True) - log_keep
        w = jnp.where(causal, jnp.exp(log_beta + log_stay), 0.0)
        outs.append(jnp.einsum('bhts,bhsd->bhtd', w.astype(vb.dtype), vb))
    o = jnp.concatenate(outs, axis=2).transpose(0, 2, 1, 3).reshape(B, S, H * hd)
    return o @ w_out

def moe_swiglu(h, w_router, w_gate, w_up, w_down):
    logits = (h @ w_router).astype(jnp.float32)
    top_val, top_idx = lax.top_k(logits, TOP_K)
    top_w = jax.nn.softmax(top_val, axis=-1)
    gates = jnp.sum(jax.nn.one_hot(top_idx, N_EXPERTS, dtype=jnp.float32) * top_w[..., None], axis=-2)
    out = jnp.zeros_like(h)
    for e in range(N_EXPERTS):
        y = swiglu(h, w_gate[e], w_up[e], w_down[e])
        out = out + gates[..., e:e + 1].astype(h.dtype) * y
    return out

def first_inputs(seed: int = 0) -> dict:
    key = jax.random.key(seed)
    ks = jax.random.split(key, 20)
    D = D_MODEL

    def w(k, shape, fan_in):
        return jax.random.normal(k, shape, dtype=jnp.float32) * (fan_in ** -0.5)

    def gain(k, shape):
        return 1.0 + 0.02 * jax.random.normal(k, shape, dtype=jnp.float32)

    return {
        "x": jax.random.normal(ks[0], (BATCH, SEQ, D), dtype=jnp.float32),
        "attn_norm": gain(ks[1], (DEPTH, D)),
        "ffn_norm": gain(ks[2], (DEPTH, D)),
        "kv_norm": gain(ks[3], (D,)),
        "final_norm": gain(ks[4], (D,)),
        "gla_w_in": w(ks[5], (N_A, D, GLA_IN), D),
        "gla_w_gate_up": w(ks[6], (N_A, GLA_GATE_RANK, GLA_QK), GLA_GATE_RANK),
        "gla_b_gate": 0.1 * jax.random.normal(ks[7], (N_A, GLA_QK), dtype=jnp.float32),
        "gla_head_norm": gain(ks[8], (N_A, GLA_DV)),
        "gla_w_out": w(ks[9], (N_A, GLA_V, D), GLA_V),
        "sb_w_kv": w(ks[10], (D, 2 * SB_HEADS * SB_HEAD_DIM), D),
        "sb_w_q": w(ks[11], (N_B, D, SB_HEADS * SB_HEAD_DIM), D),
        "sb_w_out": w(ks[12], (N_B, SB_HEADS * SB_HEAD_DIM, D), SB_HEADS * SB_HEAD_DIM),
        "ffn_w_gate": w(ks[13], (N_DENSE, D, FFN_DIM), D),
        "ffn_w_up": w(ks[14], (N_DENSE, D, FFN_DIM), D),
        "ffn_w_down": w(ks[15], (N_DENSE, FFN_DIM, D), FFN_DIM),
        "moe_w_router": w(ks[16], (N_MOE, D, N_EXPERTS), D),
        "moe_w_gate": w(ks[17], (N_MOE, N_EXPERTS, D, EXPERT_DIM), D),
        "moe_w_up": w(ks[18], (N_MOE, N_EXPERTS, D, EXPERT_DIM), D),
        "moe_w_down": w(ks[19], (N_MOE, N_EXPERTS, EXPERT_DIM, D), EXPERT_DIM),
    }

def first_block(x, attn_norm, ffn_norm, kv_norm, final_norm, gla_w_in, gla_w_gate_up, gla_b_gate,
              gla_head_norm, gla_w_out, sb_w_kv, sb_w_q, sb_w_out, ffn_w_gate, ffn_w_up, ffn_w_down,
              moe_w_router, moe_w_gate, moe_w_up, moe_w_down):
    B, S, D = x.shape
    h = x
    k_shared = None
    v_shared = None
    for layer in range(DEPTH):
        if layer < N_A:
            h = h + gla_mixer(rms_norm(h, attn_norm[layer]), gla_w_in[layer], gla_w_gate_up[layer],
                              gla_b_gate[layer], gla_head_norm[layer], gla_w_out[layer])
        else:
            if layer == N_A:
                kv = rms_norm(h, kv_norm) @ sb_w_kv
                k_s, v_s = jnp.split(kv, 2, axis=-1)
                k_shared = k_s.reshape(B, S, SB_HEADS, SB_HEAD_DIM).transpose(0, 2, 1, 3)
                v_shared = v_s.reshape(B, S, SB_HEADS, SB_HEAD_DIM).transpose(0, 2, 1, 3)
            ib = layer - N_A
            h = h + stick_breaking_mixer(rms_norm(h, attn_norm[layer]), k_shared, v_shared,
                                         sb_w_q[ib], sb_w_out[ib])
        hn = rms_norm(h, ffn_norm[layer])
        if layer % 2 == 0:
            i = layer // 2
            h = h + swiglu(hn, ffn_w_gate[i], ffn_w_up[i], ffn_w_down[i])
        else:
            i = layer // 2
            h = h + moe_swiglu(hn, moe_w_router[i], moe_w_gate[i], moe_w_up[i], moe_w_down[i])
    return rms_norm(h, final_norm)


HEAD_DIM = 64
A_HEADS = 16
A_WIDTH = A_HEADS * HEAD_DIM
DILATED_PAIRS = ((128, 1), (512, 4), (2048, 16))
B_HEADS = D_MODEL // (2 * HEAD_DIM)
B_QK_WIDTH = 2 * B_HEADS * HEAD_DIM
B_V_DIM = 2 * HEAD_DIM
B_WIDTH = B_HEADS * B_V_DIM
IN_WIDTHS = (A_WIDTH, A_WIDTH, A_WIDTH, A_WIDTH,
             B_QK_WIDTH, B_QK_WIDTH, B_WIDTH, B_WIDTH,
             D_MODEL, D_MODEL)
IN_TOTAL = sum(IN_WIDTHS)
ROPE_THETA = 500000.0
ROPE_DIM = HEAD_DIM // 4
Q_BLOCK = 128
SUBLN_EPS = 1e-5
NEG = -1e30


def rms_norm_2(x, w, eps):
    xf = x.astype(jnp.float32)
    return xf * lax.rsqrt(jnp.mean(xf * xf, axis=-1, keepdims=True) + eps) * w.astype(jnp.float32)

def rope_tables(seq):
    inv = 1.0 / (ROPE_THETA ** (jnp.arange(0, ROPE_DIM, 2, dtype=jnp.float32) / ROPE_DIM))
    ang = jnp.arange(seq, dtype=jnp.float32)[:, None] * inv[None, :]
    return jnp.cos(ang), jnp.sin(ang)

def partial_rope(t, cos, sin):
    half = ROPE_DIM // 2
    tr = t[..., :ROPE_DIM].astype(jnp.float32)
    t1, t2 = tr[..., :half], tr[..., half:]
    c = cos[None, :, None, :]
    s = sin[None, :, None, :]
    rot = jnp.concatenate([t1 * c - t2 * s, t1 * s + t2 * c], axis=-1).astype(t.dtype)
    return jnp.concatenate([rot, t[..., ROPE_DIM:]], axis=-1)

def split_cols(u):
    outs = []
    start = 0
    for w in IN_WIDTHS:
        outs.append(u[..., start:start + w])
        start += w
    return outs

def dilated_pattern(q, k, v, window, dilation):
    b, s, h, dh = q.shape
    n = window // dilation
    chunk = dilation * n
    sp = -(-s // chunk) * chunk
    length = sp // dilation
    nb = length // n

    def to_blocks(t):
        t = jnp.pad(t, ((0, 0), (0, sp - s), (0, 0), (0, 0)))
        t = t.reshape(b, length, dilation, h, dh).transpose(0, 2, 1, 3, 4)
        return t.reshape(b, dilation, nb, n, h, dh)

    def with_prev(t):
        prev = jnp.pad(t, ((0, 0), (0, 0), (1, 0), (0, 0), (0, 0), (0, 0)))[:, :, :-1]
        return jnp.concatenate([prev, t], axis=3)

    qb = to_blocks(q)
    kb = with_prev(to_blocks(k))
    vb = with_prev(to_blocks(v))
    scores = jnp.einsum('brnqhd,brnkhd->brnqhk', qb, kb,
                        preferred_element_type=jnp.float32) * (HEAD_DIM ** -0.5)
    qi = jnp.arange(n)[:, None]
    kc = jnp.arange(2 * n)[None, :]
    dist = qi + n - kc
    blk = jnp.arange(nb)[:, None, None]
    valid = (dist >= 0) & (dist <= n) & (blk * n + kc - n >= 0)
    scores = jnp.where(valid[None, None, :, :, None, :], scores, NEG)
    m = jnp.max(scores, axis=-1)
    p = jnp.exp(scores - m[..., None])
    den = jnp.sum(p, axis=-1)
    o = jnp.einsum('brnqhk,brnkhd->brnqhd', p, vb.astype(jnp.float32)) / den[..., None]

    def from_blocks(t):
        t = t.reshape((b, dilation, length) + t.shape[4:])
        t = jnp.swapaxes(t, 1, 2)
        return t.reshape((b, sp) + t.shape[3:])[:, :s]

    return from_blocks(o), from_blocks(m), from_blocks(den)

def dilated_mixture(q, k, v):
    outs = [dilated_pattern(q, k, v, w, d) for (w, d) in DILATED_PAIRS]
    m_all = jnp.stack([r[1] for r in outs])
    d_all = jnp.stack([r[2] for r in outs])
    o_all = jnp.stack([r[0] for r in outs])
    wts = d_all * jnp.exp(m_all - jnp.max(m_all, axis=0))
    return jnp.sum(wts[..., None] * o_all, axis=0) / jnp.sum(wts, axis=0)[..., None]

def diff_attention(q1, q2, k1, k2, v, lam):
    b, s, h, dh = q1.shape
    nq = s // Q_BLOCK
    qs = jnp.stack([q1, q2], 0).reshape(2, b, nq, Q_BLOCK, h, dh).transpose(2, 0, 1, 3, 4, 5)
    ks = jnp.stack([k1, k2], 0)
    vf = v.astype(jnp.float32)
    kpos = jnp.arange(s)

    def one_block(args):
        qblk, bi = args
        sc = jnp.einsum('mbqhd,mbkhd->mbhqk', qblk, ks,
                        preferred_element_type=jnp.float32) * (dh ** -0.5)
        qpos = bi * Q_BLOCK + jnp.arange(Q_BLOCK)
        sc = jnp.where(kpos[None, :] <= qpos[:, None], sc, NEG)
        p = jax.nn.softmax(sc, axis=-1)
        a = p[0] - lam * p[1]
        return jnp.einsum('bhqk,bkhe->bqhe', a, vf)

    out = lax.map(one_block, (qs, jnp.arange(nq)))
    return out.transpose(1, 0, 2, 3, 4).reshape(b, s, h, 2 * dh)

def lambda_init_value(layer):
    return 0.8 - 0.6 * math.exp(-0.3 * layer)

def hybrid_layer(x, layer, norm_w, w_in, lq1, lk1, lq2, lk2, subln_w,
                 w_proj_a, w_proj_b, w_out, cos, sin):
    b, s, _ = x.shape
    hdn = rms_norm_2(x, norm_w, RMS_EPS).astype(x.dtype)
    u = hdn @ w_in
    qa, ka, va, za, qb, kb, vb, zb, ga, gb = split_cols(u)

    qa = partial_rope(qa.reshape(b, s, A_HEADS, HEAD_DIM), cos, sin)
    ka = partial_rope(ka.reshape(b, s, A_HEADS, HEAD_DIM), cos, sin)
    va = va.reshape(b, s, A_HEADS, HEAD_DIM)
    ya = dilated_mixture(qa, ka, va).reshape(b, s, A_WIDTH)
    ya = ya * jax.nn.silu(za.astype(jnp.float32))

    qb = partial_rope(qb.reshape(b, s, 2 * B_HEADS, HEAD_DIM), cos, sin)
    kb = partial_rope(kb.reshape(b, s, 2 * B_HEADS, HEAD_DIM), cos, sin)
    vb = vb.reshape(b, s, B_HEADS, B_V_DIM)
    lam_init = lambda_init_value(layer)
    lam = (jnp.exp(jnp.sum(lq1.astype(jnp.float32) * lk1.astype(jnp.float32)))
           - jnp.exp(jnp.sum(lq2.astype(jnp.float32) * lk2.astype(jnp.float32))) + lam_init)
    ob = diff_attention(qb[:, :, 0::2], qb[:, :, 1::2], kb[:, :, 0::2], kb[:, :, 1::2], vb, lam)
    ob = rms_norm_2(ob, subln_w, SUBLN_EPS) * (1.0 - lam_init)
    yb = ob.reshape(b, s, B_WIDTH) * jax.nn.silu(zb.astype(jnp.float32))

    pa = ya.astype(x.dtype) @ w_proj_a
    pb = yb.astype(x.dtype) @ w_proj_b
    merged = (jax.nn.sigmoid(ga.astype(jnp.float32)) * pa.astype(jnp.float32)
              + jax.nn.sigmoid(gb.astype(jnp.float32)) * pb.astype(jnp.float32))
    return x + (merged.astype(x.dtype) @ w_out).astype(x.dtype)

def second_inputs(seed: int = 0) -> dict:
    key = jax.random.key(seed)
    ks = jax.random.split(key, 16)
    f32 = jnp.float32
    x = jax.random.normal(ks[0], (BATCH, SEQ, D_MODEL), f32)
    norm_w = 1.0 + 0.02 * jax.random.normal(ks[1], (DEPTH, D_MODEL), f32)
    w_in = jax.random.normal(ks[2], (DEPTH, D_MODEL, IN_TOTAL), f32) * D_MODEL ** -0.5
    lambda_q1 = 0.1 * jax.random.normal(ks[3], (DEPTH, HEAD_DIM), f32)
    lambda_k1 = 0.1 * jax.random.normal(ks[4], (DEPTH, HEAD_DIM), f32)
    lambda_q2 = 0.1 * jax.random.normal(ks[5], (DEPTH, HEAD_DIM), f32)
    lambda_k2 = 0.1 * jax.random.normal(ks[6], (DEPTH, HEAD_DIM), f32)
    subln_w = 1.0 + 0.02 * jax.random.normal(ks[7], (DEPTH, B_V_DIM), f32)
    w_proj_a = jax.random.normal(ks[8], (DEPTH, A_WIDTH, D_MODEL), f32) * A_WIDTH ** -0.5
    w_proj_b = jax.random.normal(ks[9], (DEPTH, B_WIDTH, D_MODEL), f32) * B_WIDTH ** -0.5
    w_out = jax.random.normal(ks[10], (DEPTH, D_MODEL, D_MODEL), f32) * D_MODEL ** -0.5
    final_norm_w = 1.0 + 0.02 * jax.random.normal(ks[11], (D_MODEL,), f32)
    return {'x': x, 'norm_w': norm_w, 'w_in': w_in,
            'lambda_q1': lambda_q1, 'lambda_k1': lambda_k1,
            'lambda_q2': lambda_q2, 'lambda_k2': lambda_k2,
            'subln_w': subln_w, 'w_proj_a': w_proj_a, 'w_proj_b': w_proj_b,
            'w_out': w_out, 'final_norm_w': final_norm_w}

def second_block(x, norm_w, w_in, lambda_q1, lambda_k1, lambda_q2, lambda_k2,
              subln_w, w_proj_a, w_proj_b, w_out, final_norm_w):
    cos, sin = rope_tables(x.shape[1])
    h = x
    for layer in range(DEPTH):
        h = hybrid_layer(h, layer, norm_w[layer], w_in[layer],
                         lambda_q1[layer], lambda_k1[layer], lambda_q2[layer], lambda_k2[layer],
                         subln_w[layer], w_proj_a[layer], w_proj_b[layer], w_out[layer],
                         cos, sin)
    return rms_norm_2(h, final_norm_w, RMS_EPS).astype(x.dtype)


def setup_inputs(seed=0):
    out = dict(first_inputs(seed))
    for name, value in second_inputs(seed + 1).items():
        if name != "x":
            out[name + "_2"] = value
    return out


def reference(
    x, attn_norm, ffn_norm, kv_norm, final_norm, gla_w_in, gla_w_gate_up, gla_b_gate,
    gla_head_norm, gla_w_out, sb_w_kv, sb_w_q, sb_w_out, ffn_w_gate, ffn_w_up, ffn_w_down,
    moe_w_router, moe_w_gate, moe_w_up, moe_w_down, norm_w_2, w_in_2, lambda_q1_2, lambda_k1_2,
    lambda_q2_2, lambda_k2_2, subln_w_2, w_proj_a_2, w_proj_b_2, w_out_2, final_norm_w_2,
):
    x = first_block(
        x, attn_norm, ffn_norm, kv_norm, final_norm, gla_w_in, gla_w_gate_up, gla_b_gate,
        gla_head_norm, gla_w_out, sb_w_kv, sb_w_q, sb_w_out, ffn_w_gate, ffn_w_up, ffn_w_down,
        moe_w_router, moe_w_gate, moe_w_up, moe_w_down,
    )
    return second_block(
        x, norm_w_2, w_in_2, lambda_q1_2, lambda_k1_2, lambda_q2_2, lambda_k2_2, subln_w_2,
        w_proj_a_2, w_proj_b_2, w_out_2, final_norm_w_2,
    )


_drawn_inputs = setup_inputs


def setup_inputs(seed=0):
    import zlib

    import numpy as np

    out = dict(_drawn_inputs(seed))
    spreads = {}
    factors = {'norm_w_2': 3.996, 'lambda_k1_2': 3.127, 'subln_w_2': 8.0}
    for name, (base, spread) in spreads.items():
        noise = np.random.default_rng([zlib.crc32(name.encode()), seed]).standard_normal(out[name].shape)
        drawn = base * np.exp(spread * noise) if base else spread * noise
        out[name] = jnp.asarray(drawn.astype(out[name].dtype))
    for name, factor in factors.items():
        out[name] = (out[name] * factor).astype(out[name].dtype)
    return out
```

```python
from contextlib import ExitStack

import concourse.bass as bass
from concourse import mybir

F32 = mybir.dt.float32
F32R = mybir.dt.float32r
I32 = mybir.dt.int32
ALU = mybir.AluOpType
ACT = mybir.ActivationFunctionType
AX = mybir.AxisListType.X

P = 128
D = 1024
S = 256
TT = S // P
KC = D // P
EPS = 1e-6
SUB_EPS = 1e-5

GLA_H, GLA_DK, GLA_DV, GLA_C, GLA_RANK = 4, 128, 256, 64, 16
GLA_QK, GLA_V = GLA_H * GLA_DK, GLA_H * GLA_DV
N_CHUNK = S // GLA_C
GATE_NORM = 16.0

SB_H, SB_HD = 8, 128
FFN_DIM = 2816
N_EXPERTS, EXPERT_DIM = 8, 3584
FC = 256
FFN_STEPS = FFN_DIM // FC
MOE_STEPS = EXPERT_DIM // FC
CAP = P

A_H, A_HD = 16, 64
B_H, B_HD = 8, 64
NEG = -1e30

SLOT = 4 * 512
SPLIT = 3
RING, RING_WIDE = 2, 4
MOE_RING = 7

G_ATTN0, G_FFN0, G_KV, G_ATTN1, G_FFN1, G_HY0, G_HY1 = (KC * i for i in range(7))
G_BGATE = 7 * KC
G_HEAD = G_BGATE + GLA_H
G_SUB = G_HEAD + 2
N_GAINS = G_SUB + 2

_CONST = [("ident", P), ("glamask", P), ("later", P), ("ones", P), ("sbmask", 384), ("upto", P), ("slots", 2 * P),
          ("causal", 384), ("dilneg", 384), ("dilcount", 384), ("cos", 16), ("sin", 16), ("before", 64)]
C_AT, _n = {}, 0
for _name, _w in _CONST:
    C_AT[_name] = (_n, _w)
    _n += _w
N_CONST = _n


class Sem:

    def __init__(self, nc, ctx, name):
        self.sem = ctx.enter_context(nc.semaphore(name))
        self.base = 0

    def at(self, n):
        return self.base + n

    def close(self, n):
        self.base += n


class Stream:

    def __init__(self, nc, ctx, prefix, high, low):
        self.nc, self.ctx, self.prefix, self.high, self.low = nc, ctx, prefix, high, low
        self.rounded = ctx.enter_context(nc.semaphore(prefix + "rounded"))
        self.split = ctx.enter_context(nc.semaphore(prefix + "split"))
        self.used = ctx.enter_context(nc.semaphore(prefix + "used"))
        self.landing = {}
        self.landed = {}
        self.last = {}
        self.tiles = []
        self.parts = {}
        self.issued = 0
        self.cursor = {"act": 0, "dve": 0}
        self.taken = 0
        self.slot = 0

    def sem(self, slot):
        if slot not in self.landing:
            self.landing[slot] = self.ctx.enter_context(self.nc.semaphore(f"{self.prefix}landed_{slot}"))
            self.landed[slot] = 0
        return self.landing[slot]

    def plan(self, slots, parts_of):
        name, memory = slots[self.slot % len(slots)]
        self.slot += 1
        n = len(self.tiles)
        self.sem(name)
        parts = parts_of(memory)
        self.parts[n] = (parts, self.last[name] + 1 if name in self.last else 0)
        self.last[name] = n
        self.landed[name] += 16 * len(parts)
        self.tiles.append((memory, name, self.landed[name]))
        return n

    def ahead(self):
        return min(self.taken + SPLIT - 1, len(self.tiles))

    def issue(self, sync, splits=None):
        splits = self.ahead() if splits is None else splits
        while self.issued < len(self.tiles) and self.parts[self.issued][1] <= splits:
            parts, need = self.parts.pop(self.issued)
            if need:
                sync.wait_ge(self.split, need)
            for dst, src in parts:
                sync.dma_start(dst, src).then_inc(self.landing[self.tiles[self.issued][1]], 16)
            self.issued += 1

    def round_tile(self, act, place, memory, landed, value, before):
        act.wait_ge(landed, value)
        if before is not None:
            act.wait_ge(self.used, before)
        self.nc.scalar.activation(self.high[:, place, :], memory, ACT.Copy).then_inc(self.rounded, 1)

    def rest_of_tile(self, dve, place, memory, rounded):
        dve.wait_ge(self.rounded, rounded)
        self.nc.vector.tensor_tensor(self.low[:, place, :], memory, self.high[:, place, :].bitcast(F32), ALU.subtract).then_inc(self.split, 1)

    def prepare(self, eng, who, upto):
        while self.cursor[who] < min(upto, self.ahead()):
            n = self.cursor[who]
            memory, name, value = self.tiles[n]
            if who == "act":
                self.round_tile(eng, n % SPLIT, memory, self.landing[name], value, n - SPLIT + 1 if n >= SPLIT else None)
            else:
                self.rest_of_tile(eng, n % SPLIT, memory, n + 1)
            self.cursor[who] += 1

    def operand(self, place, cols):
        return self.high[:, place, cols], self.low[:, place, cols]


def matmul3(nc, out, x, w, start, stop, **more):
    nc.tensor.matmul(out, x[0], w[0], start=start, stop=False, **more)
    nc.tensor.matmul(out, x[0], w[1], start=False, stop=False, **more)
    return nc.tensor.matmul(out, x[1], w[0], start=False, stop=stop, **more)


class Core:
    pass


def build(nc, I, out, stop=None, cap=CAP):
    with ExitStack() as ctx:
        K = Core()
        K.nc, K.I, K.ctx, K.cap = nc, I, ctx, cap

        def sb(name, shape, dt=F32):
            return ctx.enter_context(nc.sbuf_tensor(name, shape, dt))

        K.h = sb("h", [P, TT, D])
        K.xT = (sb("xT_high", [P, KC, S], F32R), sb("xT_low", [P, KC, S], F32R))
        K.xn = sb("xn", [P, TT, D])
        K.ring = sb("ring", [P, RING, SLOT])
        high, low = sb("w_high", [P, SPLIT, SLOT], F32R), sb("w_low", [P, SPLIT, SLOT], F32R)
        K.consts = sb("consts_sb", [P, N_CONST])
        K.gains = sb("gains_sb", [P, N_GAINS])
        K.stat = sb("stat", [P, 4, 2])
        K.bank = [ctx.enter_context(nc.psum_tensor(f"bank{i}", [P, 512], F32)) for i in range(8)]
        K.W = Stream(nc, ctx, "w_", high, low)
        K.s_in, K.s_consts = Sem(nc, ctx, "x_loaded"), ctx.enter_context(nc.semaphore("consts_loaded"))
        K.sumsq, K.var, K.std, K.rstd, K.scaled, K.xT_psum, K.xT_gained, K.xT_high, K.xT_low, K.mm, K.evac_act, K.evac_dve = (
            Sem(nc, ctx, n) for n in ("sumsq", "var", "std", "rstd", "scaled", "xT_psum", "xT_gained", "xT_rounded", "xT_rest",
                                      "matmul", "evac_act", "evac_dve"))
        K.norms = 0
        K.row_in = Sem(nc, ctx, "row_loaded")
        K.hy = {n: Sem(nc, ctx, "hy_" + n) for n in (
            "roped", "roped_b", "qk_turned", "q_out", "k_out", "score", "masked", "exp", "weights", "turned", "pT", "values", "silu",
            "first_out", "lam_dot", "lam_exp", "lam", "chain", "chain_b", "values_out", "squared", "head_var", "head_std", "yb", "sigmoid",
            "product", "merged")}
        K.const = lambda name: K.consts[:, C_AT[name][0]:C_AT[name][0] + C_AT[name][1]]
        K.ident = K.const("ident")

        K.slots = [(i, K.ring[:, i, :]) for i in range(RING)]
        before_hybrid = ctx.enter_context(ExitStack())
        wide = before_hybrid.enter_context(nc.sbuf_tensor("ring_wide", [P, RING_WIDE - RING, SLOT], F32))
        K.slots_wide = K.slots + [(RING + i, wide[:, i, :]) for i in range(RING_WIDE - RING)]
        plan_weights(K)
        load_inputs(K)
        gla(K)
        if stop != "gla":
            ffn(K)
        if stop not in ("gla", "ffn"):
            stick_breaking(K)
        if stop not in ("gla", "ffn", "sb"):
            moe(K)
        before_hybrid.close()
        if stop not in ("gla", "ffn", "sb", "moe"):
            K.W.slot = 0
            plan_hybrid(K, 0)
            final_norm(K, "final_norm")
            if stop != "mid":
                hybrid(K, 0)
            if stop not in ("mid", "hy0"):
                hybrid(K, 1)
                final_norm(K, "final_norm_w_2")
        store(K, out)


def load_inputs(K):
    with K.nc.Block() as block:
        @block.sync
        def _(sync):
            sync.dma_start(K.h[:], K.I["x"].rearrange("b (t p) d -> p (b t) d", p=P)).then_inc(K.s_in.sem, 16)
            sync.dma_start(K.gains[:], K.I["gains"]).then_inc(K.s_consts, 16)
            sync.dma_start(K.consts[:], K.I["consts"]).then_inc(K.s_consts, 16)
            K.W.issue(sync, 0)
            sync.wait_ge(K.s_in.sem, 16)


def store(K, out):
    with K.nc.Block() as block:
        @block.sync
        def _(sync):
            s = K.s_in.at(16)
            sync.dma_start(out.rearrange("b (t p) d -> p (b t) d", p=P), K.h[:]).then_inc(K.s_in.sem, 16)
            sync.wait_ge(K.s_in.sem, s + 16)


def proj_parts(src, k0, c, width=512):
    return lambda dst: [(dst.rearrange("p (k n) -> p k n", k=4), src[:, k0:k0 + 4, bass.ds(c, width)])]


def plan_proj(K, w, cols, slots):
    src = w.rearrange("(k p) n -> p k n", p=P)
    blocks = []
    for c in cols:
        blocks.append(K.W.plan(slots, proj_parts(src, 0, c)))
        K.W.plan(slots, proj_parts(src, 4, c))
    return blocks


def step_order(n):
    order = [("guA", 0), ("guB", 0)]
    for c in range(1, n):
        order += [("guA", c), ("guB", c), ("dn", c - 1)]
    return order + [("dn", n - 1)]


def step_parts(weights, kind, c):
    w_gate, w_up, w_down = weights
    if kind == "dn":
        return lambda dst: [(dst.rearrange("p (j n) -> p j n", j=2), w_down[c * FC:(c + 1) * FC, :].rearrange("(j p) n -> p j n", p=P))]
    k0 = 0 if kind == "guA" else 4

    def parts(dst):
        d = dst.rearrange("p (k n) -> p k n", k=4)
        return [(d[:, :, i * FC:(i + 1) * FC], w.rearrange("(k p) n -> p k n", p=P)[:, k0:k0 + 4, c * FC:(c + 1) * FC])
                for i, w in enumerate((w_gate, w_up))]
    return parts


def plan_weights(K):
    I, q, wide = K.I, GLA_QK, K.slots_wide
    r0 = 2 * q + GLA_V + GLA_RANK
    K.t_gla = plan_proj(K, I["gla_w_in"][0], [0, q, 2 * q, 2 * q + 512, r0, r0 + 512], wide)
    K.t_gla_out = plan_proj(K, I["gla_w_out"][0], [0, 512], wide)
    ffn_w = (I["ffn_w_gate"][0], I["ffn_w_up"][0], I["ffn_w_down"][0])
    K.t_ffn = {u: K.W.plan(wide, step_parts(ffn_w, *u)) for u in step_order(FFN_STEPS)}
    K.t_sb = []
    for c in (0, 512):
        K.t_sb.append(plan_proj(K, I["sb_w_kv"], [c], wide) + plan_proj(K, I["sb_w_q"][0], [c], wide) + plan_proj(K, I["sb_w_kv"], [D + c], wide))
    K.t_sb_out = plan_proj(K, I["sb_w_out"][0], [0, 512], wide)


def load_sqrt(K):
    K.nc.scalar.activation(K.stat[:, 2, :], K.const("ones")[:, 0:2], ACT.Sqrt)


def square_sums(K, eng):
    t = 0 if eng is K.nc.scalar else 1
    out, h, total = K.xn[:, t, :], K.h[:, t, :], K.stat[:, 0, t:t + 1]
    if t == 0:
        eng.activation(out, h, ACT.Square, accum_out=total).then_inc(K.sumsq.sem, 1)
    else:
        eng.tensor_tensor_reduce(out=out, in0=h, in1=h, scale=1.0, scalar=0.0, op0=ALU.mult, op1=ALU.add, accum_out=total).then_inc(K.sumsq.sem, 1)


def norm_transpose(K, targets, loads=lambda sync: None, inputs=None, tile=1):
    nc = K.nc
    nt = len(targets)
    K.norms += 1
    with nc.sbuf_tensor(f"gained{K.norms}", [P, nt, 4, 512], F32) as gained, nc.Block() as block:
        @block.sync
        def _(sync):
            loads(sync)
            K.W.issue(sync, K.W.cursor["dve"])

        @block.scalar
        def _(act):
            square_sums(K, nc.scalar)
            act.wait_ge(K.var.sem, K.var.at(1))
            nc.scalar.activation(K.stat[:, 2, :], K.stat[:, 1, :], ACT.Sqrt).then_inc(K.std.sem, 1)
            K.W.prepare(act, "act", K.W.taken + tile)
            for i in range(4):
                for j, (_, dst) in enumerate(targets):
                    act.wait_ge(K.xT_gained.sem, K.xT_gained.at(nt * i + j + 1))
                    nc.scalar.activation(dst[0][:, 4 * (i % 2):4 * (i % 2) + 4, (i // 2) * P:(i // 2 + 1) * P],
                                         gained[:, j, i, :].rearrange("p (k n) -> p k n", k=4), ACT.Copy).then_inc(K.xT_high.sem, 1)

        @block.vector
        def _(dve):
            square_sums(K, nc.vector)
            dve.wait_ge(K.sumsq.sem, K.sumsq.at(TT))
            nc.vector.tensor_scalar(K.stat[:, 1, :], K.stat[:, 0, :], 1.0 / D, EPS, ALU.mult, ALU.add).then_inc(K.var.sem, 1)
            dve.wait_ge(K.std.sem, K.std.at(1))
            nc.vector.reciprocal(K.stat[:, 3, :], K.stat[:, 2, :]).then_inc(K.rstd.sem, 1)
            dve.wait_ge(K.rstd.sem, K.rstd.at(1))
            for t in range(TT):
                nc.vector.tensor_scalar(K.xn[:, t, :], K.h[:, t, :], K.stat[:, 3, t:t + 1], None,
                                        ALU.mult).then_inc(K.scaled.sem, 1)
            K.W.prepare(dve, "dve", K.W.taken + tile)
            if inputs:
                dve.wait_ge(*inputs)
            for i in range(4):
                dve.wait_ge(K.xT_psum.sem, K.xT_psum.at(i + 1))
                for j, (g, _) in enumerate(targets):
                    gain = K.gains[:, g + 4 * (i % 2):g + 4 * (i % 2) + 4].unsqueeze(2).broadcast_to([P, 4, P])
                    nc.vector.tensor_tensor(gained[:, j, i, :].rearrange("p (k n) -> p k n", k=4),
                                            K.bank[i][:].rearrange("p (k n) -> p k n", k=4), gain, ALU.mult).then_inc(K.xT_gained.sem, 1)
            for i in range(4):
                for j, (_, dst) in enumerate(targets):
                    dve.wait_ge(K.xT_high.sem, K.xT_high.at(nt * i + j + 1))
                    where = (slice(None), slice(4 * (i % 2), 4 * (i % 2) + 4), slice((i // 2) * P, (i // 2 + 1) * P))
                    nc.vector.tensor_tensor(dst[1][where], gained[:, j, i, :].rearrange("p (k n) -> p k n", k=4),
                                            dst[0][where].bitcast(F32), ALU.subtract).then_inc(K.xT_low.sem, 1)

        @block.tensor
        def _(pe):
            if inputs:
                pe.wait_ge(*inputs)
            for t in range(TT):
                pe.wait_ge(K.scaled.sem, K.scaled.at(t + 1))
                for hf in range(2):
                    for j in range(4):
                        last = nc.tensor.transpose(K.bank[2 * t + hf][:, j * P:(j + 1) * P],
                                                   K.xn[:, t, (4 * hf + j) * P:(4 * hf + j + 1) * P], K.ident)
                    last.then_inc(K.xT_psum.sem, 1)

    for s, n in ((K.sumsq, TT), (K.var, 1), (K.std, 1), (K.rstd, 1), (K.scaled, TT), (K.xT_psum, 4), (K.xT_gained, 4 * nt),
                 (K.xT_high, 4 * nt), (K.xT_low, 4 * nt)):
        s.close(n)


def project(K, blocks, lhs, dst=None):
    nc, W = K.nc, K.W
    n, first = len(blocks), W.taken
    assert blocks[0] == first
    W.taken += 2 * n
    lhs = lhs if isinstance(lhs, list) else [lhs] * n
    add = dst is None
    if add:
        dst = lambda j, t: K.h[:, t, 512 * j:512 * (j + 1)]
    with nc.Block() as block:
        @block.sync
        def _(sync):
            W.issue(sync)

        @block.tensor
        def _(pe):
            for j in range(n):
                for half in range(2):
                    tile = first + 2 * j + half
                    pe.wait_ge(W.split, tile + 1)
                    for t, evac in enumerate((K.evac_act, K.evac_dve)):
                        if j >= 2 and half == 0:
                            pe.wait_ge(evac.sem, evac.at(j - 1))
                        last = block_half(nc, K.bank[(2 * j + t) % 4], lhs[j], W, tile % SPLIT, t, half)
                        if t == 1:
                            last.then_inc(W.used, 1)
                        elif half == 1:
                            last.then_inc(K.mm.sem, 1)

        @block.scalar
        def _(act):
            W.prepare(act, "act", first + SPLIT)
            for j in range(n):
                W.prepare(act, "act", first + 2 * j + 1 + SPLIT)
                if not add:
                    act.wait_ge(K.mm.sem, K.mm.at(j + 1))
                    nc.scalar.activation(dst(j, 0), K.bank[(2 * j) % 4][:], ACT.Copy).then_inc(K.evac_act.sem, 1)
                W.prepare(act, "act", first + 2 * j + 2 + SPLIT)
            if add:
                load_sqrt(K)

        @block.vector
        def _(dve):
            W.prepare(dve, "dve", first + SPLIT)
            for j in range(n):
                W.prepare(dve, "dve", first + 2 * j + 1 + SPLIT)
                if add:
                    dve.wait_ge(K.mm.sem, K.mm.at(j + 1))
                    nc.vector.tensor_tensor(dst(j, 0), K.bank[(2 * j) % 4][:], dst(j, 0), ALU.add).then_inc(K.evac_act.sem, 1)
                dve.wait_ge(W.used, first + 2 * j + 2)
                b = K.bank[(2 * j + 1) % 4]
                if add:
                    nc.vector.tensor_tensor(dst(j, 1), b[:], dst(j, 1), ALU.add).then_inc(K.evac_dve.sem, 1)
                else:
                    nc.vector.tensor_copy(dst(j, 1), b[:]).then_inc(K.evac_dve.sem, 1)
                W.prepare(dve, "dve", first + 2 * j + 2 + SPLIT)

    for s in (K.mm, K.evac_act, K.evac_dve):
        s.close(n)


def block_half(nc, bank, lhs, W, place, t, half):
    for k in range(4):
        kk = 4 * half + k
        last = matmul3(nc, bank[:], tuple(x[:, kk, t * P:(t + 1) * P] for x in lhs), W.operand(place, slice(k * 512, (k + 1) * 512)),
                       start=(kk == 0), stop=(kk == KC - 1))
    return last


def transposes(nc, K, bank, srcs, width=P):
    for j, src in enumerate(srcs):
        last = nc.tensor.transpose(bank[:, j * width:(j + 1) * width], src, K.ident)
    return last


def gla(K):
    nc = K.nc
    with ExitStack() as ctx:
        def sb(name, shape):
            return ctx.enter_context(nc.sbuf_tensor(name, shape, F32))

        def sem(name):
            return ctx.enter_context(nc.semaphore(name))

        U = sb("gla_u", [P, TT, 2 * GLA_QK + 2 * GLA_V])
        w_lr = sb("gla_w_lr", [P, KC, GLA_RANK])
        w_up = sb("gla_w_up", [GLA_RANK, GLA_QK])
        reset = sb("gla_reset", [P, GLA_H * S])
        s_small = sem("gla_small_loaded")

        def loads(sync):
            c0 = 2 * GLA_QK + GLA_V
            src = K.I["gla_w_in"][0].rearrange("(k p) n -> p k n", p=P)
            with nc.allow_non_contiguous_dma(reason="16 columns of a row"):
                sync.dma_start(w_lr[:], src[:, :, c0:c0 + GLA_RANK]).then_inc(s_small, 16)
            sync.dma_start(w_up[:], K.I["gla_w_gate_up"][0]).then_inc(s_small, 16)
            sync.dma_start(reset[:], K.I["reset"].partition_broadcast(P)).then_inc(s_small, 16)

        norm_transpose(K, [(G_ATTN0, K.xT)], loads, (K.s_consts, 32))

        project(K, K.t_gla[:4], K.xT, lambda j, t: U[:, t, 512 * j:512 * (j + 1)])

        q = lambda t, h: U[:, t, h * P:(h + 1) * P]
        k = lambda t, h: U[:, t, GLA_QK + h * P:GLA_QK + (h + 1) * P]
        v = lambda t, h: U[:, t, 2 * GLA_QK + h * GLA_DV:2 * GLA_QK + (h + 1) * GLA_DV]
        r = U[:, :, 2 * GLA_QK + GLA_V:]
        lrT = sb("gla_lrT", [GLA_RANK, S])
        za = sb("gla_z", [P, GLA_H, S])
        ab = sb("gla_abs", [P, GLA_H, S])
        eb = sb("gla_eb", [P, GLA_H, S])
        enb = sb("gla_enb", [P, GLA_H, S])
        qd = sb("gla_qd", [P, GLA_H, S])
        ki = sb("gla_ki", [P, GLA_H, S])
        ke = sb("gla_ke", [P, GLA_H, S])
        kend = sb("gla_kend", [P, TT, GLA_QK])
        aT = sb("gla_aT", [P, TT, GLA_H, P])
        state = sb("gla_state", [P, N_CHUNK - 1, GLA_H, GLA_DV])
        hs = sb("gla_headstat", [P, 4, TT * GLA_H])
        gained = [U[:, i // 2, 512 * (i % 2):512 * (i % 2 + 1)].rearrange("p (k n) -> p k n", k=4) for i in range(4)]
        flat = lambda x: x[:].rearrange("p h s -> p (h s)")
        B = K.bank
        pair = lambda b: b[:].rearrange("p (h s) -> p h s", h=2)
        quad = lambda b: b[:].rearrange("p (h s) -> p h s", h=4)
        ev = {n: sem("gla_" + n) for n in ("lr", "lrT", "gate", "z", "ln", "b", "exp", "end", "endexp", "qT", "qd", "keT",
                                           "kend", "attn", "aT", "kv", "state", "silu", "o", "osq", "ovar", "ostd",
                                           "orstd", "og", "ogT", "oT", "oT_high", "oT_low", "chain_a", "chain_v")}

        beside = Beside(K, K.t_gla[4:], lambda j, t: r[:, t, 512 * j:512 * (j + 1)], (B[4], B[7]))
        with nc.Block() as block:
            @block.sync
            def _(sync):
                K.W.issue(sync)

            @block.tensor
            def _(pe):
                pe.wait_ge(s_small, 48)
                for c in range(KC):
                    for i, x in enumerate(K.xT):
                        last = nc.tensor.matmul(B[4][0:GLA_RANK, 0:S], w_lr[:, c, :], x[:, c, :].bitcast(F32),
                                                start=(c == 0 and i == 0), stop=(c == KC - 1 and i == 1))
                last.then_inc(ev["lr"], 1)
                for bank, src in ((0, q), (1, q), (2, k), (3, k)):
                    hh = 2 * (bank % 2)
                    transposes(nc, K, B[bank], [src(t, hh + g) for g in range(2) for t in range(TT)]).then_inc(ev["qT"], 1)
                pe.wait_ge(ev["lrT"], 1)
                for hd in range(GLA_H):
                    last = nc.tensor.matmul(pair(B[5 + hd // 2])[:, hd % 2, :], w_up[:, hd * P:(hd + 1) * P], lrT[:], start=True, stop=True)
                last.then_inc(ev["gate"], 1)
                for tile in range(2 * beside.n):
                    beside.pe(pe, tile)
                pe.wait_ge(ev["qd"], 2)
                for t in range(TT):
                    for hd in range(GLA_H):
                        ts_ = slice(t * P, (t + 1) * P)
                        last = nc.tensor.matmul(quad(B[5 + t])[:, hd, :], ki[:, hd, ts_], qd[:, hd, ts_], start=True, stop=True)
                    last.then_inc(ev["attn"], 1)
                pe.wait_ge(ev["qd"], 3)
                for evac in (K.evac_act, K.evac_dve):
                    pe.wait_ge(evac.sem, evac.at(beside.n))
                for t, bank in ((0, 4), (1, 7)):
                    transposes(nc, K, B[bank], [ke[:, hd, t * P:(t + 1) * P] for hd in range(GLA_H)]).then_inc(ev["keT"], 1)
                pe.wait_ge(ev["kend"], 2)
                for n, banks in ((0, (0, 1)), (1, (2, 3)), (2, (4, 7))):
                    t, rows = n // 2, slice((n % 2) * GLA_C, (n % 2 + 1) * GLA_C)
                    for hd in range(GLA_H):
                        last = nc.tensor.matmul(pair(B[banks[hd // 2]])[:, hd % 2, :], kend[rows, t, hd * P:(hd + 1) * P],
                                                v(t, hd)[rows, :], start=True, stop=True)
                    last.then_inc(ev["kv"], 1)
                pe.wait_ge(ev["aT"], TT)
                pe.wait_ge(ev["state"], 3 * GLA_H)
                for t in range(TT):
                    for hd in range(GLA_H):
                        o = pair(B[2 * t + hd // 2])[:, hd % 2, :]
                        last = nc.tensor.matmul(o, aT[:, t, hd, :], v(t, hd), start=True, stop=True, skip_group_check=True)
                        for half in range(2):
                            n = 2 * t + half
                            if n:
                                rows = slice(half * GLA_C, (half + 1) * GLA_C)
                                last = nc.tensor.matmul(o[rows, :], qd[:, hd, n * GLA_C:(n + 1) * GLA_C], state[:, n - 1, hd, :],
                                                        start=False, stop=True, skip_group_check=True)
                    last.then_inc(ev["o"], 1)
                for t in range(TT):
                    pe.wait_ge(ev["og"], GLA_H * (t + 1))
                    for hf in range(2):
                        transposes(nc, K, B[4 + 2 * t + hf], [K.xn[:, t, (4 * hf + j) * P:(4 * hf + j + 1) * P] for j in range(4)]).then_inc(ev["ogT"], 1)

            @block.scalar
            def _(act):
                n = 0

                def then(ins):
                    nonlocal n
                    n += 1
                    ins.then_inc(ev["chain_a"], 1)
                    act.wait_ge(ev["chain_a"], n)

                K.W.prepare(act, "act", beside.first + SPLIT)
                act.wait_ge(ev["z"], 1)
                then(nc.scalar.activation(flat(ab), flat(za), ACT.Abs))
                then(nc.scalar.activation(flat(ab), flat(ab), ACT.Exp, scale=-1.0))
                nc.scalar.activation(flat(ab), flat(ab), ACT.Ln, bias=1.0).then_inc(ev["ln"], 1)
                beside.act(act, 0)
                act.wait_ge(ev["b"], 1)
                nc.scalar.activation(flat(eb), flat(ab), ACT.Exp, scale=1.0 / GATE_NORM).then_inc(ev["exp"], 1)
                nc.scalar.activation(flat(enb), flat(ab), ACT.Exp, scale=-1.0 / GATE_NORM).then_inc(ev["exp"], 1)
                beside.act(act, 1)
                act.wait_ge(ev["end"], 1)
                nc.scalar.activation(flat(za), flat(za), ACT.Exp, scale=1.0 / GATE_NORM).then_inc(ev["endexp"], 1)
                beside.act(act, 2)
                beside.act(act, 3)
                for t, bank in ((0, 4), (1, 7)):
                    act.wait_ge(ev["keT"], t + 1)
                    nc.scalar.activation(kend[:, t, :], B[bank][:], ACT.Copy).then_inc(ev["kend"], 1)
                act.wait_ge(K.evac_dve.sem, K.evac_dve.at(beside.n))
                act.wait_ge(K.evac_act.sem, K.evac_act.at(beside.n))
                nc.scalar.activation(r, r, ACT.Silu).then_inc(ev["silu"], 1)
                for t in range(TT):
                    act.wait_ge(ev["o"], t + 1)
                    for hd in range(GLA_H):
                        nc.scalar.activation(K.xn[:, t, hd * GLA_DV:(hd + 1) * GLA_DV], pair(B[2 * t + hd // 2])[:, hd % 2, :], ACT.Square,
                                             accum_out=hs[:, 0, t * GLA_H + hd:t * GLA_H + hd + 1]).then_inc(ev["osq"], 1)
                act.wait_ge(ev["ovar"], 1)
                nc.scalar.activation(hs[:, 2, :], hs[:, 1, :], ACT.Sqrt).then_inc(ev["ostd"], 1)
                for i in range(4):
                    act.wait_ge(ev["oT"], 2 * i + 2)
                    nc.scalar.activation(K.xT[0][:, 4 * (i % 2):4 * (i % 2) + 4, (i // 2) * P:(i // 2 + 1) * P], gained[i],
                                         ACT.Copy).then_inc(ev["oT_high"], 1)

            @block.vector
            def _(dve):
                n = 0

                def then(ins):
                    nonlocal n
                    n += 1
                    ins.then_inc(ev["chain_v"], 1)
                    dve.wait_ge(ev["chain_v"], n)

                K.W.prepare(dve, "dve", beside.first + SPLIT)
                dve.wait_ge(s_small, 48)
                dve.wait_ge(ev["lr"], 1)
                nc.vector.tensor_copy(lrT[:], B[4][0:GLA_RANK, 0:S]).then_inc(ev["lrT"], 1)
                dve.wait_ge(ev["gate"], 1)
                for g in range(2):
                    bias = K.gains[:, G_BGATE + 2 * g:G_BGATE + 2 * g + 2].unsqueeze(2).broadcast_to([P, 2, S])
                    ins = nc.vector.tensor_tensor(za[:, 2 * g:2 * g + 2, :], pair(B[5 + g]), bias, ALU.add)
                    if g == 0:
                        then(ins)
                ins.then_inc(ev["z"], 1)
                dve.wait_ge(ev["ln"], 1)
                dve.wait_ge(ev["z"], 1)
                then(nc.vector.scalar_tensor_tensor(out=flat(za), in0=flat(za), scalar=0.0, in1=flat(ab), op0=ALU.min, op1=ALU.subtract))
                nc.vector.tensor_tensor_scan(flat(ab), reset[:], flat(za), 0.0, ALU.mult, ALU.add).then_inc(ev["b"], 1)
                dve.wait_ge(ev["b"], 1)
                ch = lambda x: flat(x).rearrange("p (n c) -> p n c", c=GLA_C)
                nc.vector.tensor_tensor(ch(za), ch(ab)[:, :, GLA_C - 1:GLA_C].broadcast_to([P, GLA_H * N_CHUNK, GLA_C]), ch(ab),
                                        ALU.subtract).then_inc(ev["end"], 1)
                beside.dve(dve, 0)
                dve.wait_ge(ev["qT"], 2)
                dve.wait_ge(ev["exp"], 1)
                sl = lambda x, g: x[:, 2 * g:2 * g + 2, :].rearrange("p h s -> p (h s)")
                for g in range(2):
                    ins = nc.vector.scalar_tensor_tensor(out=sl(qd, g), in0=B[g][:], scalar=GLA_DK ** -0.5, in1=sl(eb, g), op0=ALU.mult, op1=ALU.mult)
                    if g == 0:
                        then(ins)
                ins.then_inc(ev["qd"], 1)
                dve.wait_ge(ev["qT"], 4)
                dve.wait_ge(ev["exp"], 2)
                for g in range(2):
                    ins = nc.vector.tensor_tensor(sl(ki, g), B[2 + g][:], sl(enb, g), ALU.mult)
                    if g == 0:
                        then(ins)
                ins.then_inc(ev["qd"], 1)
                beside.dve(dve, 1)
                dve.wait_ge(ev["endexp"], 1)
                for g in range(2):
                    ins = nc.vector.tensor_tensor(sl(ke, g), B[2 + g][:], sl(za, g), ALU.mult)
                    if g == 0:
                        then(ins)
                ins.then_inc(ev["qd"], 1)
                beside.dve(dve, 2)
                beside.dve(dve, 3)
                for t in range(TT):
                    dve.wait_ge(ev["attn"], t + 1)
                    nc.vector.tensor_tensor(aT[:, t, :, :], quad(B[5 + t]), K.const("glamask").unsqueeze(1).broadcast_to([P, GLA_H, P]),
                                            ALU.mult).then_inc(ev["aT"], 1)
                for n_, banks in ((0, (0, 1)), (1, (2, 3)), (2, (4, 7))):
                    dve.wait_ge(ev["kv"], n_ + 1)
                    if n_:
                        dve.wait_ge(ev["state"], n_ * GLA_H)
                    for hd in range(GLA_H):
                        kv = pair(B[banks[hd // 2]])[:, hd % 2, :]
                        if n_ == 0:
                            ins = nc.vector.tensor_copy(state[:, 0, hd, :], kv)
                        else:
                            c = n_ * GLA_C + GLA_C - 1
                            ins = nc.vector.scalar_tensor_tensor(out=state[:, n_, hd, :], in0=state[:, n_ - 1, hd, :], scalar=eb[:, hd, c:c + 1],
                                                                 in1=kv, op0=ALU.mult, op1=ALU.add)
                        ins.then_inc(ev["state"], 1)
                dve.wait_ge(ev["osq"], TT * GLA_H)
                nc.vector.tensor_scalar(hs[:, 1, :], hs[:, 0, :], 1.0 / GLA_DV, EPS, ALU.mult, ALU.add).then_inc(ev["ovar"], 1)
                dve.wait_ge(ev["ostd"], 1)
                then(nc.vector.reciprocal(hs[:, 3, :], hs[:, 2, :]))
                dve.wait_ge(ev["silu"], 1)
                for t in range(TT):
                    for hd in range(GLA_H):
                        i = t * GLA_H + hd
                        nc.vector.scalar_tensor_tensor(out=K.xn[:, t, hd * GLA_DV:(hd + 1) * GLA_DV], in0=pair(B[2 * t + hd // 2])[:, hd % 2, :],
                                                       scalar=hs[:, 3, i:i + 1], in1=r[:, t, hd * GLA_DV:(hd + 1) * GLA_DV],
                                                       op0=ALU.mult, op1=ALU.mult).then_inc(ev["og"], 1)
                gain = K.gains[:, G_HEAD:G_HEAD + 2].unsqueeze(2).broadcast_to([P, 2, P])
                for i in range(4):
                    dve.wait_ge(ev["ogT"], i + 1)
                    for g in range(2):
                        ins = nc.vector.tensor_tensor(gained[i][:, 2 * g:2 * g + 2, :], quad(B[4 + i])[:, 2 * g:2 * g + 2, :], gain, ALU.mult)
                        ins.then_inc(ev["oT"], 1)
                for i in range(4):
                    where = (slice(None), slice(4 * (i % 2), 4 * (i % 2) + 4), slice((i // 2) * P, (i // 2 + 1) * P))
                    dve.wait_ge(ev["oT_high"], i + 1)
                    nc.vector.tensor_tensor(K.xT[1][where], gained[i], K.xT[0][where].bitcast(F32), ALU.subtract).then_inc(ev["oT_low"], 1)

        beside.close()
        project(K, K.t_gla_out, K.xT)


def ffn(K):
    nc, W, B = K.nc, K.W, K.bank
    norm_transpose(K, [(G_FFN0, K.xT)])
    N, first = FFN_STEPS, W.taken
    W.taken += 3 * N
    number = K.t_ffn
    with ExitStack() as ctx:
        sg = ctx.enter_context(nc.sbuf_tensor("ffn_silu", [P, 2, TT, FC], F32))
        hid = ctx.enter_context(nc.sbuf_tensor("ffn_hidden", [P, 2, TT, FC], F32))
        hT = [ctx.enter_context(nc.sbuf_tensor("ffn_hiddenT_" + n, [P, 2, 2, S], F32R)) for n in ("high", "low")]
        s_gu, s_silu, s_hid, s_tp, s_high, s_hT = (ctx.enter_context(nc.semaphore("ffn_" + n)) for n in
                                                   ("gu0", "silu", "hidden", "hiddenT_psum", "hiddenT_rounded", "hiddenT"))
        with nc.Block() as block:
            @block.sync
            def _(sync):
                W.issue(sync)

            @block.tensor
            def _(pe):
                def gate_up(c, half):
                    tile = number["guB" if half else "guA", c]
                    pe.wait_ge(W.split, tile + 1)
                    for t in range(TT):
                        if c and half == 0:
                            pe.wait_ge(s_hid, 2 * (c - 1) + t + 1)
                        last = block_half(nc, B[4 + t], K.xT, W, tile % SPLIT, t, half)
                        if t == 1:
                            last.then_inc(W.used, 1)
                        elif half:
                            last.then_inc(s_gu, 1)

                def turn(c):
                    pe.wait_ge(s_hid, 2 * c + 2)
                    if c >= 2:
                        pe.wait_ge(s_hT, c - 1)
                    transposes(nc, K, B[6 + c % 2], [hid[:, c % 2, t, f * P:(f + 1) * P] for f in range(2) for t in range(TT)]).then_inc(s_tp, 1)

                def down(c):
                    tile = number["dn", c]
                    pe.wait_ge(W.split, tile + 1)
                    pe.wait_ge(s_hT, c + 1)
                    for t in range(TT):
                        for f in range(2):
                            for n in range(2):
                                last = matmul3(nc, B[2 * t + n][:], tuple(x[:, c % 2, f, t * P:(t + 1) * P] for x in hT),
                                               W.operand(tile % SPLIT, slice(f * D + n * 512, f * D + (n + 1) * 512)),
                                               start=(c == 0 and f == 0), stop=(c == N - 1 and f == 1))
                    last.then_inc(W.used, 1)

                for c in range(N):
                    gate_up(c, 0)
                    if c:
                        turn(c - 1)
                    gate_up(c, 1)
                    if c:
                        down(c - 1)
                turn(N - 1)
                down(N - 1)

            @block.scalar
            def _(act):
                def high_turned(c):
                    act.wait_ge(s_tp, c + 1)
                    if c >= 2:
                        act.wait_ge(W.used, number["dn", c - 2] + 1)
                    nc.scalar.activation(hT[0][:, c % 2, :, :].rearrange("p f s -> p (f s)"), B[6 + c % 2][:], ACT.Copy).then_inc(s_high, 1)

                W.prepare(act, "act", first + SPLIT)
                for c in range(N):
                    if c:
                        high_turned(c - 1)
                    W.prepare(act, "act", number["guA", c] + 1 + SPLIT)
                    for t in range(TT):
                        if t == 0:
                            act.wait_ge(s_gu, c + 1)
                        else:
                            act.wait_ge(W.used, number["guB", c] + 1)
                        if c >= 2:
                            act.wait_ge(s_hid, 2 * (c - 2) + t + 1)
                        nc.scalar.activation(sg[:, c % 2, t, :], B[4 + t][:, 0:FC], ACT.Silu).then_inc(s_silu, 1)
                    W.prepare(act, "act", number["guB", c] + 1 + SPLIT)
                    if c:
                        W.prepare(act, "act", number["dn", c - 1] + 1 + SPLIT)
                high_turned(N - 1)
                W.prepare(act, "act", W.ahead())
                load_sqrt(K)

            @block.vector
            def _(dve):
                def low_turned(c):
                    dve.wait_ge(s_high, c + 1)
                    flat = [x[:, c % 2, :, :].rearrange("p f s -> p (f s)") for x in hT]
                    nc.vector.tensor_tensor(flat[1], B[6 + c % 2][:], flat[0].bitcast(F32), ALU.subtract).then_inc(s_hT, 1)

                W.prepare(dve, "dve", first + SPLIT)
                for c in range(N):
                    if c:
                        low_turned(c - 1)
                    W.prepare(dve, "dve", number["guA", c] + 1 + SPLIT)
                    for t in range(TT):
                        dve.wait_ge(s_silu, 2 * c + t + 1)
                        if c >= 2:
                            dve.wait_ge(s_tp, c - 1)
                        nc.vector.tensor_tensor(hid[:, c % 2, t, :], sg[:, c % 2, t, :], B[4 + t][:, FC:2 * FC], ALU.mult).then_inc(s_hid, 1)
                    W.prepare(dve, "dve", number["guB", c] + 1 + SPLIT)
                    if c:
                        W.prepare(dve, "dve", number["dn", c - 1] + 1 + SPLIT)
                low_turned(N - 1)
                dve.wait_ge(W.used, first + 3 * N)
                for t in range(TT):
                    for n in range(2):
                        hv = K.h[:, t, n * 512:(n + 1) * 512]
                        nc.vector.tensor_tensor(hv, B[2 * t + n][:], hv, ALU.add).then_inc(K.evac_dve.sem, 1)
                W.prepare(dve, "dve", W.ahead())
    K.evac_dve.close(4)


def staged(n, stages):
    for i in range(n + max(lag for lag, _ in stages)):
        for lag, f in stages:
            if 0 <= i - lag < n:
                f(i - lag)


def stick_breaking(K):
    nc, B, W = K.nc, K.bank, K.W
    W3 = 3 * P
    with ExitStack() as ctx:
        def sb(name, shape):
            return ctx.enter_context(nc.sbuf_tensor(name, shape, F32))

        def sem(name):
            return ctx.enter_context(nc.semaphore("sb_" + name))

        xq = tuple(ctx.enter_context(nc.sbuf_tensor("sb_xq_" + n, [P, KC, S], F32R)) for n in ("high", "low"))
        norm_transpose(K, [(G_KV, K.xT), (G_ATTN1, xq)])
        U = sb("sb_u", [P, TT, 3 * D])
        lhs = [K.xT, xq, K.xT]
        project(K, K.t_sb[0], lhs, lambda j, t: U[:, t, D * j:D * j + 512])
        kT, qT = sb("sb_kT", [P, SB_H, S]), sb("sb_qT", [P, SB_H, S])
        la = sb("sb_la", [P, 2, 2, W3])
        keep = sb("sb_keep", [P, 2, 2, W3])
        mw = sb("sb_mw", [P, 2, 2, W3])
        beta = sb("sb_beta", [P, 2, 2, W3])
        e = {n: sem(n) for n in ("turned", "q_out", "k_out", "z", "abs", "expn", "ln", "zp", "keep", "mkeep", "beta", "stay", "logw", "expw",
                                 "w", "o", "oT_high", "oT")}
        SC = SB_HD ** -0.5
        beside = Beside(K, K.t_sb[1], lambda j, t: U[:, t, D * j + 512:D * (j + 1)], (B[6], B[7]), lhs)
        order = [("turn", 0), ("score", 0), ("tile", 0), ("turn", 1), ("tile", 1), ("score", 1), ("stay", 0), ("tile", 2), ("stay", 1),
                 ("tile", 3), ("values", 0), ("turn", 2), ("score", 2), ("tile", 4), ("values", 1), ("turn", 3), ("score", 3),
                 ("tile", 5), ("stay", 2), ("stay", 3), ("values", 2), ("values", 3)]
        oT = xq
        assert order.index(("values", 0)) > order.index(("tile", 3))
        flat = lambda x, i: x[:, i % 2, :, :].rearrange("p h w -> p (h w)")
        mask2 = K.const("sbmask").unsqueeze(1).broadcast_to([P, 2, W3])

        def walk(**parts):
            for what, i in order:
                parts[what](i)

        with nc.Block() as block:
            @block.sync
            def _(sync):
                W.issue(sync)

            @block.tensor
            def _(pe):
                def turn(i):
                    if i == 2:
                        pe.wait_ge(K.evac_act.sem, K.evac_act.at(2))
                        pe.wait_ge(K.evac_dve.sem, K.evac_dve.at(2))
                    if i >= 2:
                        pe.wait_ge(e["oT"], i - 1)
                    if i:
                        pe.wait_ge(e["q_out"], i)
                        pe.wait_ge(e["k_out"], i)
                    for b, at in ((5, D), (4, 0)):
                        transposes(nc, K, B[b], [U[:, t, at + hd * P:at + (hd + 1) * P] for hd in (2 * i, 2 * i + 1) for t in range(TT)]).then_inc(e["turned"], 1)

                def score(i):
                    pe.wait_ge(e["q_out"], i + 1)
                    pe.wait_ge(e["k_out"], i + 1)
                    if i:
                        pe.wait_ge(e["beta"], 2 * i)
                    for g in range(2):
                        z, h = B[g], 2 * i + g
                        nc.tensor.matmul(z[:, 0:S], kT[:, h, 0:P], qT[:, h, :], start=True, stop=True)
                        nc.tensor.matmul(z[:, S:W3], kT[:, h, P:S], qT[:, h, P:S], start=True, stop=True).then_inc(e["z"], 1)

                def stay(i):
                    pe.wait_ge(e["mkeep"], i + 1)
                    if i:
                        pe.wait_ge(e["logw"], 2 * i)
                    for g in range(2):
                        b, m = B[2 + g], mw[:, i % 2, g, :]
                        nc.tensor.matmul(b[:, 0:S], K.const("later"), m[:, 0:S], start=True, stop=True, skip_group_check=True)
                        nc.tensor.matmul(b[:, P:S], K.const("ones"), m[:, S:W3], start=False, stop=True, skip_group_check=True)
                        nc.tensor.matmul(b[:, S:W3], K.const("later"), m[:, S:W3], start=True, stop=True, skip_group_check=True).then_inc(e["stay"], 1)

                def values(i):
                    pe.wait_ge(e["w"], i + 1)
                    pe.wait_ge(e["k_out"], min(i + 2, 4))
                    if i:
                        pe.wait_ge(e["oT"], i)
                    if i == 2:
                        pe.wait_ge(K.evac_act.sem, K.evac_act.at(3))
                        pe.wait_ge(K.evac_dve.sem, K.evac_dve.at(3))
                    for g in range(2):
                        h, b, x = 2 * i + g, B[4][:, g * S:(g + 1) * S], mw[:, i % 2, g, :]
                        v = U[:, :, 2 * D + h * P:2 * D + (h + 1) * P]
                        nc.tensor.matmul(b, v[:, 0, :], x[:, 0:S], start=True, stop=True, skip_group_check=True)
                        last = nc.tensor.matmul(b[:, P:S], v[:, 1, :], x[:, S:W3], start=False, stop=True, skip_group_check=True)
                    last.then_inc(e["o"], 1)

                walk(turn=turn, score=score, stay=stay, values=values, tile=lambda v: beside.pe(pe, v))

            @block.scalar
            def _(act):
                def turn(i):
                    act.wait_ge(e["turned"], 2 * i + 1)
                    nc.scalar.activation(qT[:, 2 * i:2 * i + 2, :].rearrange("p h s -> p (h s)"), B[5][:], ACT.Copy).then_inc(e["q_out"], 1)

                def score(i):
                    for g in range(2):
                        act.wait_ge(e["z"], 2 * i + g + 1)
                        if i >= 2:
                            act.wait_ge(e["keep"], i - 1)
                        nc.scalar.activation(la[:, i % 2, g, :], B[g][:, 0:W3], ACT.Abs, scale=SC).then_inc(e["abs"], 1)
                    act.wait_ge(e["abs"], 2 * i + 2)
                    nc.scalar.activation(flat(la, i), flat(la, i), ACT.Exp, scale=-1.0).then_inc(e["expn"], 1)
                    act.wait_ge(e["expn"], i + 1)
                    nc.scalar.activation(flat(la, i), flat(la, i), ACT.Ln, bias=1.0).then_inc(e["ln"], 1)

                def stay(i):
                    act.wait_ge(e["logw"], 2 * i + 2)
                    nc.scalar.activation(flat(beta, i), flat(beta, i), ACT.Exp).then_inc(e["expw"], 1)

                def values(i):
                    act.wait_ge(e["o"], i + 1)
                    nc.scalar.activation(oT[0][:, 2 * i:2 * i + 2, :].rearrange("p h s -> p (h s)"), B[4][:], ACT.Copy).then_inc(e["oT_high"], 1)

                W.prepare(act, "act", beside.first + SPLIT)
                walk(turn=turn, score=score, stay=stay, values=values, tile=lambda v: beside.act(act, v))

            @block.vector
            def _(dve):
                def turn(i):
                    dve.wait_ge(e["turned"], 2 * i + 2)
                    nc.vector.tensor_copy(kT[:, 2 * i:2 * i + 2, :].rearrange("p h s -> p (h s)"), B[4][:]).then_inc(e["k_out"], 1)

                def score(i):
                    dve.wait_ge(e["abs"], 2 * i + 2)
                    if i >= 2:
                        dve.wait_ge(e["beta"], 2 * i - 2)
                    for g in range(2):
                        ins = nc.vector.tensor_scalar(keep[:, i % 2, g, :], B[g][:, 0:W3], SC, 0.0, ALU.mult, ALU.max)
                    ins.then_inc(e["zp"], 1)
                    dve.wait_ge(e["zp"], i + 1)
                    dve.wait_ge(e["ln"], i + 1)
                    nc.vector.scalar_tensor_tensor(out=flat(keep, i), in0=flat(keep, i), scalar=-1.0, in1=flat(la, i),
                                                   op0=ALU.mult, op1=ALU.subtract).then_inc(e["keep"], 1)
                    dve.wait_ge(e["keep"], i + 1)
                    if i >= 2:
                        dve.wait_ge(e["o"], i - 1)
                    nc.vector.tensor_tensor(mw[:, i % 2, :, :], keep[:, i % 2, :, :], mask2, ALU.mult).then_inc(e["mkeep"], 1)
                    if i >= 2:
                        dve.wait_ge(e["w"], i - 1)
                    for g in range(2):
                        nc.vector.scalar_tensor_tensor(out=beta[:, i % 2, g, :], in0=B[g][:, 0:W3], scalar=SC, in1=keep[:, i % 2, g, :],
                                                       op0=ALU.mult, op1=ALU.add).then_inc(e["beta"], 1)

                def stay(i):
                    dve.wait_ge(e["beta"], 2 * i + 2)
                    for g in range(2):
                        dve.wait_ge(e["stay"], 2 * i + g + 1)
                        nc.vector.tensor_tensor(beta[:, i % 2, g, :], beta[:, i % 2, g, :], B[2 + g][:, 0:W3], ALU.add).then_inc(e["logw"], 1)
                    dve.wait_ge(e["expw"], i + 1)
                    nc.vector.tensor_tensor(mw[:, i % 2, :, :], beta[:, i % 2, :, :], mask2, ALU.mult).then_inc(e["w"], 1)

                def values(i):
                    dve.wait_ge(e["oT_high"], i + 1)
                    high, low = (x[:, 2 * i:2 * i + 2, :].rearrange("p h s -> p (h s)") for x in oT)
                    nc.vector.tensor_tensor(low, B[4][:], high.bitcast(F32), ALU.subtract).then_inc(e["oT"], 1)

                W.prepare(dve, "dve", beside.first + SPLIT)
                walk(turn=turn, score=score, stay=stay, values=values, tile=lambda v: beside.dve(dve, v))

        beside.close()
        project(K, K.t_sb_out, oT)


def expert_weights(K, e):
    one = lambda w: w[0][bass.ds(e, 1)].rearrange("e k n -> (e k) n")
    return one(K.I["moe_w_gate"]), one(K.I["moe_w_up"]), one(K.I["moe_w_down"])


class ExpertSems:

    def __init__(self, nc, ctx, prefix, stream, first, value, start):
        (self.sel, self.gath, self.xt, self.xh, self.xg, self.silu, self.hid, self.tp, self.hh, self.hT, self.ya, self.yv, self.gps,
         self.gst, self.sc, self.add) = (
            ctx.enter_context(nc.semaphore(prefix + n)) for n in
            ("chosen", "gathered", "gained", "x_rounded", "x", "silu", "hidden", "hiddenT_psum", "hiddenT_rounded", "hiddenT", "y_act",
             "y_dve", "gateT_psum", "gateT", "scattered", "added"))
        self.stream, self.first = stream, first
        self.value = value
        self.start = start


def moe(K):
    nc, W, B = K.nc, K.W, K.bank
    E, N = N_EXPERTS, MOE_STEPS
    order = step_order(N)
    PER = len(order)
    number = {u: i for i, u in enumerate(order)}
    assert PER % MOE_RING == 0 and PER % SPLIT == 0
    with ExitStack() as ctx:
        def sb(name, shape, dt=F32):
            return ctx.enter_context(nc.sbuf_tensor("moe_" + name, shape, dt))

        extra = sb("ring", [P, MOE_RING - RING_WIDE, SLOT])
        slots = K.slots_wide + [(RING_WIDE + i, extra[:, i, :]) for i in range(MOE_RING - RING_WIDE)]
        first = len(W.tiles)
        W.slot = 0
        for u in order:
            W.plan(slots, step_parts(expert_weights(K, 0), *u))
        run0 = W.tiles[first:]
        per_slot = {}
        for kind, c in order:
            name = run0[number[kind, c]][1]
            per_slot[name] = per_slot.get(name, 0) + (16 if kind == "dn" else 32)
        w_router = sb("w_router", [P, KC, E])
        router_in = ctx.enter_context(nc.semaphore("moe_router_loaded"))
        norm_transpose(K, [(G_FFN1, K.xT)], lambda sync: sync.dma_start(
            w_router[:], K.I["moe_w_router"][0].rearrange("(k p) n -> p k n", p=P)).then_inc(router_in, 16), tile=0)

        posm = sb("slot_of", [P, TT, E + 1])
        gate = sb("gate", [P, TT, E + 1])
        table = sb("table", [1, 2 * E + 1], I32)
        sel = sb("sel", [P, TT, P])
        gsel = sb("gsel", [P, TT, P])
        gselT = sb("gselT", [P, S])
        xt = sb("x_gained", [P, KC, P])
        xg = (sb("x_high", [P, KC, P], F32R), sb("x_low", [P, KC, P], F32R))
        sg = sb("silu", [P, 2, FC])
        hid = sb("hidden", [P, 2, FC])
        hT = (sb("hiddenT_high", [P, 2, 2 * P], F32R), sb("hiddenT_low", [P, 2, 2 * P], F32R))
        y = sb("y", [P, D])

        route(K, posm, gate, table, w_router, router_in)

        G = ExpertSems(nc, ctx, "moe_", W, first, lambda u, n: (W.landing[run0[u][1]], n * per_slot[run0[u][1]] + run0[u][2]), 1)

        def make_sel(dve, G, e, slot_numbers):
            for t in range(TT):
                nc.vector.tensor_scalar(sel[:, t, :], slot_numbers, posm[:, t, bass.ds(e, 1)], None, ALU.is_equal)
                ins = nc.vector.tensor_scalar(gsel[:, t, :], slot_numbers, posm[:, t, bass.ds(e, 1)], gate[:, t, bass.ds(e, 1)], ALU.is_equal, ALU.mult)
            ins.then_inc(G.sel, 1)

        def gather(pe, G, n):
            pe.wait_ge(G.sel, n + 1)
            for k in range(KC):
                for t in range(TT):
                    last = nc.tensor.matmul(B[2 + k // 4][:, (k % 4) * P:(k % 4 + 1) * P], K.xn[:, t, k * P:(k + 1) * P], sel[:, t, :],
                                            start=(t == 0), stop=(t == TT - 1))
                if k % 4 == 3:
                    last.then_inc(G.gath, 1)

        def gathered_act(act, G, n):
            for g in range(2):
                act.wait_ge(G.xt, 2 * n + g + 1)
                nc.scalar.activation(xg[0][:, 4 * g:4 * g + 4, :], xt[:, 4 * g:4 * g + 4, :], ACT.Copy).then_inc(G.xh, 1)

        def gathered_dve(dve, G, n):
            for g in range(2):
                dve.wait_ge(G.gath, 2 * n + g + 1)
                gain = K.gains[:, G_FFN1 + 4 * g:G_FFN1 + 4 * g + 4].unsqueeze(2).broadcast_to([P, 4, P])
                nc.vector.tensor_tensor(xt[:, 4 * g:4 * g + 4, :], B[2 + g][:].rearrange("p (k n) -> p k n", k=4), gain, ALU.mult).then_inc(G.xt, 1)
            for g in range(2):
                dve.wait_ge(G.xh, 2 * n + g + 1)
                nc.vector.tensor_tensor(xg[1][:, 4 * g:4 * g + 4, :], xt[:, 4 * g:4 * g + 4, :], xg[0][:, 4 * g:4 * g + 4, :].bitcast(F32),
                                        ALU.subtract).then_inc(G.xg, 1)

        def scatter(pe, G, m):
            for s_ in (G.ya, G.yv, G.gst):
                pe.wait_ge(s_, m + 1)
            for i, b in enumerate((2, 3, 7, 6)):
                t, half = i // 2, i % 2
                nc.tensor.matmul(B[b][:], gselT[:, t * P:(t + 1) * P], y[:, half * 512:(half + 1) * 512], start=True, stop=True).then_inc(G.sc, 1)

        def scattered(dve, G, m):
            for i, b in enumerate((2, 3, 7, 6)):
                t, half = i // 2, i % 2
                dve.wait_ge(G.sc, 4 * m + i + 1)
                hv = K.h[:, t, half * 512:(half + 1) * 512]
                nc.vector.tensor_tensor(hv, B[b][:], hv, ALU.add).then_inc(G.add, 1)

        def round_tile(act, G, n, u):
            at = G.first + u
            G.stream.round_tile(act, at % SPLIT, run0[u % PER][0], *G.value(u % PER, n + u // PER), n * PER + (at - SPLIT + 1))

        def rest_of_tile(dve, G, n, u):
            at = G.first + u
            G.stream.rest_of_tile(dve, at % SPLIT, run0[u % PER][0], n * PER + (at + 1))

        def pe_run(pe, G, n, first_step, late):
            F = G.stream

            def gate_up(c, half):
                at = G.first + number["guB" if half else "guA", c]
                pe.wait_ge(F.split, n * PER + (at + 1))
                if half == 0 and c == 0:
                    pe.wait_ge(G.xg, 2 * n + 2)
                elif half == 0 and c >= 2:
                    pe.wait_ge(G.hid, n * N + c - 1)
                for k in range(4):
                    kk = 4 * half + k
                    last = matmul3(nc, B[4 + c % 2][:], (xg[0][:, kk, :], xg[1][:, kk, :]), F.operand(at % SPLIT, slice(k * 512, (k + 1) * 512)),
                                   start=(kk == 0), stop=(kk == KC - 1))
                last.then_inc(F.used, 1)

            def turn(c):
                pe.wait_ge(G.hid, n * N + c + 1)
                transposes(nc, K, B[6][:, (c % 2) * S:(c % 2 + 1) * S], [hid[:, c % 2, f * P:(f + 1) * P] for f in range(2)]).then_inc(G.tp, 1)

            def down(c):
                at = G.first + number["dn", c]
                pe.wait_ge(F.split, n * PER + (at + 1))
                pe.wait_ge(G.hT, n * N + c + 1)
                for f in range(2):
                    for half in range(2):
                        last = matmul3(nc, B[half][:], tuple(x[:, c % 2, f * P:(f + 1) * P] for x in hT),
                                       F.operand(at % SPLIT, slice(f * D + half * 512, f * D + (half + 1) * 512)),
                                       start=(c == 0 and f == 0), stop=(c == N - 1 and f == 1))
                last.then_inc(F.used, 1)

            for c in range(N):
                gate_up(c, 0)
                if c:
                    turn(c - 1)
                gate_up(c, 1)
                if c == 0:
                    first_step()
                if c == N - 1:
                    late()
                if c:
                    down(c - 1)
                if c == 2:
                    if G.start:
                        pe.wait_ge(G.add, 4 * n + 4)
                    transposes(nc, K, B[7], [gsel[:, t, :] for t in range(TT)]).then_inc(G.gps, 1)
            turn(N - 1)
            down(N - 1)

        def act_run(act, G, n, last_tile, late):
            def used(kind, c):
                return n * PER + (G.first + number[kind, c] + 1)

            def split(u):
                if u + SPLIT < last_tile:
                    round_tile(act, G, n, u + SPLIT)

            def turned(c):
                act.wait_ge(G.tp, n * N + c + 1)
                if c >= 2:
                    act.wait_ge(G.stream.used, used("dn", c - 2))
                nc.scalar.activation(hT[0][:, c % 2, :], B[6][:, (c % 2) * S:(c % 2 + 1) * S], ACT.Copy).then_inc(G.hh, 1)

            for c in range(N):
                if c:
                    turned(c - 1)
                split(number["guA", c])
                act.wait_ge(G.stream.used, used("guB", c))
                if c >= 2:
                    act.wait_ge(G.hid, n * N + c - 1)
                nc.scalar.activation(sg[:, c % 2, :], B[4 + c % 2][:, 0:FC], ACT.Silu).then_inc(G.silu, 1)
                if c == N - 1:
                    late()
                    turned(c)
                split(number["guB", c])
                if c:
                    split(number["dn", c - 1])
            act.wait_ge(G.stream.used, used("dn", N - 1))
            if G.start:
                act.wait_ge(G.sc, 4 * n + 4)
            nc.scalar.activation(y[:, 0:512], B[0][:], ACT.Copy).then_inc(G.ya, 1)
            split(number["dn", N - 1])

        def dve_run(dve, G, n, last_tile, first_step, third_step, late):
            def split(u):
                if u + SPLIT < last_tile:
                    rest_of_tile(dve, G, n, u + SPLIT)

            def turned(c):
                dve.wait_ge(G.hh, n * N + c + 1)
                nc.vector.tensor_tensor(hT[1][:, c % 2, :], B[6][:, (c % 2) * S:(c % 2 + 1) * S], hT[0][:, c % 2, :].bitcast(F32),
                                        ALU.subtract).then_inc(G.hT, 1)

            for c in range(N):
                if c:
                    turned(c - 1)
                split(number["guA", c])
                if c == 0:
                    first_step()
                dve.wait_ge(G.silu, n * N + c + 1)
                if c >= 2:
                    dve.wait_ge(G.tp, n * N + c - 1)
                nc.vector.tensor_tensor(hid[:, c % 2, :], sg[:, c % 2, :], B[4 + c % 2][:, FC:2 * FC], ALU.mult).then_inc(G.hid, 1)
                if c == N - 1:
                    late()
                    turned(c)
                split(number["guB", c])
                if c:
                    split(number["dn", c - 1])
                if c == 2:
                    dve.wait_ge(G.gps, n + 1)
                    nc.vector.tensor_copy(gselT[:], B[7][:, 0:S]).then_inc(G.gst, 1)
                    third_step()
            dve.wait_ge(G.stream.used, n * PER + (G.first + PER))
            nc.vector.tensor_copy(y[:, 512:], B[1][:]).then_inc(G.yv, 1)
            split(number["dn", N - 1])

        slot_numbers = K.const("slots")
        W.taken += PER
        with nc.Block() as block:
            @block.sync
            def _(sync):
                def load(weights, e, tiles):
                    for kind, c in tiles:
                        u = number[kind, c]
                        sync.wait_ge(W.split, e * PER + (first + u - MOE_RING + 1))
                        for dst, src in step_parts(weights, kind, c)(run0[u][0]):
                            sync.dma_start(dst, src).then_inc(W.landing[run0[u][1]], 16)

                W.issue(sync, first + PER)
                with sync.Fori(1, E) as e:
                    load(expert_weights(K, e), e, order)
                load(expert_weights(K, 0), E, order[:SPLIT])

            @block.tensor
            def _(pe):
                gather(pe, G, 0)
                with pe.Fori(0, E) as e:
                    pe_run(pe, G, e, lambda: scatter(pe, G, e), lambda: gather(pe, G, e + 1))
                scatter(pe, G, E)
                pe.sem_inc(W.used, SPLIT)

            @block.scalar
            def _(act):
                gathered_act(act, G, 0)
                W.prepare(act, "act", first + SPLIT)
                with act.Fori(0, E) as e:
                    act_run(act, G, e, PER + SPLIT, lambda: gathered_act(act, G, e + 1))

            @block.vector
            def _(dve):
                make_sel(dve, G, 0, slot_numbers[:, 0:P])
                nc.vector.memset(y[:, 0:512], 0.0).then_inc(G.ya, 1)
                nc.vector.memset(y[:, 512:], 0.0).then_inc(G.yv, 1)
                nc.vector.memset(gselT[:], 0.0).then_inc(G.gst, 1)
                gathered_dve(dve, G, 0)
                W.prepare(dve, "dve", first + SPLIT)
                with dve.Fori(0, E) as e:
                    dve_run(dve, G, e, PER + SPLIT, lambda: scattered(dve, G, e), lambda: make_sel(dve, G, e + 1, slot_numbers[:, 0:P]),
                            lambda: gathered_dve(dve, G, e + 1))
                scattered(dve, G, E)

        for name, n in per_slot.items():
            W.landed[name] += n * (E - 1)
        for u in order[:SPLIT]:
            W.landed[run0[number[u]][1]] += 16 if u[0] == "dn" else 32
        W.tiles += [None] * (PER * (E - 1) + SPLIT)
        W.taken = W.issued = W.cursor["act"] = W.cursor["dve"] = len(W.tiles)
        for name in per_slot:
            W.last[name] = len(W.tiles) - 1
        moe_overflow(K, ctx, table, order, number, slots, run0, expert_weights, lambda dve, G, e: make_sel(dve, G, e, slot_numbers[:, P:2 * P]),
                     gather, gathered_act, gathered_dve, scatter, scattered, round_tile, rest_of_tile, pe_run, act_run, dve_run)


def moe_overflow(K, ctx, table, order, number, slots, run0, expert_weights, make_sel, gather, gathered_act, gathered_dve, scatter, scattered,
                 round_tile, rest_of_tile, pe_run, act_run, dve_run):
    nc, E, PER = K.nc, N_EXPERTS, len(order)
    F = Stream(nc, ctx, "over_", K.W.high, K.W.low)
    landed, per_slot = [], {}
    for i, (kind, c) in enumerate(order):
        name = run0[i][1]
        F.sem(name)
        per_slot[name] = per_slot.get(name, 0) + (16 if kind == "dn" else 32)
        landed.append(per_slot[name])
    finished = ctx.enter_context(nc.semaphore("over_finished"))
    left = ctx.enter_context(nc.semaphore("over_left"))
    G = ExpertSems(nc, ctx, "over_", F, 0, lambda u, n: (F.landing[run0[u][1]], n * per_slot[run0[u][1]] + landed[u]), 0)

    def each(eng, body):
        some = eng.value_load(table[0:1, 2 * E:2 * E + 1], min_val=0, max_val=3)
        with eng.If(some > 0):
            with eng.Fori(0, E) as e:
                more = eng.value_load(table[0:1, bass.ds(e, 1)], min_val=0, max_val=1)
                n = eng.value_load(table[0:1, bass.ds(e + E, 1)], min_val=0, max_val=3)
                with eng.If(more > 0):
                    body(e, n)

    with nc.Block() as block:
        @block.sync
        def _(sync):
            def body(e, n):
                weights = expert_weights(K, e)
                for u, (kind, c) in enumerate(order):
                    if u >= MOE_RING:
                        sync.wait_ge(F.split, n * PER + (u - MOE_RING + 1))
                    for dst, src in step_parts(weights, kind, c)(run0[u][0]):
                        sync.dma_start(dst, src).then_inc(F.landing[run0[u][1]], 16)
                sync.wait_ge(finished, n + 1)
                sync.sem_inc(left, 1)
            each(sync, body)

        @block.tensor
        def _(pe):
            def body(e, n):
                gather(pe, G, n)
                pe_run(pe, G, n, lambda: None, lambda: None)
                scatter(pe, G, n)
                pe.wait_ge(finished, n + 1)
            each(pe, body)

        @block.scalar
        def _(act):
            def body(e, n):
                for u in range(SPLIT):
                    F.round_tile(act, u, run0[u][0], *G.value(u, n), None)
                gathered_act(act, G, n)
                act_run(act, G, n, PER, lambda: None)
                act.wait_ge(finished, n + 1)
                act.sem_inc(left, 1)
            each(act, body)

        @block.vector
        def _(dve):
            def body(e, n):
                make_sel(dve, G, e)
                for u in range(SPLIT):
                    rest_of_tile(dve, G, n, u)
                gathered_dve(dve, G, n)
                dve_run(dve, G, n, PER, lambda: None, lambda: None, lambda: None)
                scattered(dve, G, n)
                dve.wait_ge(G.add, 4 * n + 4)
                dve.sem_inc(finished, 1)
            each(dve, body)


def route(K, posm, gate, table, w_router, router_in):
    nc, B, E = K.nc, K.bank, N_EXPERTS
    with ExitStack() as ctx:
        def sb(name, shape):
            return ctx.enter_context(nc.sbuf_tensor("route_" + name, shape, F32))

        wr = [ctx.enter_context(nc.sbuf_tensor("route_w_" + n, [P, KC, E], F32R)) for n in ("high", "low")]
        lg = sb("logits", [P, TT, E])
        ahead = sb("ahead", [P, TT, E, E])
        tie = sb("tie", [P, TT, E, E])
        rank = sb("rank", [P, TT, E])
        ch = sb("chosen", [P, TT, E])
        ex = sb("exp", [P, TT, E])
        st = sb("stat", [P, 3, TT])
        ct = sb("counts", [1, 4, E])
        s_high, s_low, s_mm, s_ch, s_d, s_ex, v = (ctx.enter_context(nc.semaphore("route_" + n)) for n in
                                         ("w_rounded", "w_rest", "matmuls", "chosen", "shifted", "exp", "chain"))
        with nc.Block() as block:
            @block.sync
            def _(sync):
                K.W.issue(sync, K.W.cursor["dve"])

            @block.tensor
            def _(pe):
                pe.wait_ge(s_low, 1)
                for t in range(TT):
                    for k in range(KC):
                        last = matmul3(nc, B[0][:, t * E:(t + 1) * E], tuple(x[:, k, t * P:(t + 1) * P] for x in K.xT),
                                       tuple(w[:, k, :] for w in wr), start=(k == 0), stop=(k == KC - 1))
                last.then_inc(s_mm, 1)
                pe.wait_ge(s_ch, 1)
                nc.tensor.matmul(B[1][:, 0:E], K.const("upto"), ch[:, 0, :], start=True, stop=True)
                nc.tensor.matmul(B[1][:, E:2 * E], K.const("upto"), ch[:, 1, :], start=True, stop=False)
                nc.tensor.matmul(B[1][:, E:2 * E], K.const("ones"), ch[:, 0, :], start=False, stop=True)
                for t in range(TT):
                    last = nc.tensor.matmul(B[2][0:1, 0:E], K.const("ones")[:, 0:1], ch[:, t, :], start=(t == 0), stop=(t == 1))
                last.then_inc(s_mm, 1)

            @block.scalar
            def _(act):
                act.wait_ge(router_in, 16)
                nc.scalar.activation(wr[0][:], w_router[:], ACT.Copy).then_inc(s_high, 1)
                K.W.prepare(act, "act", K.W.ahead())
                act.wait_ge(s_d, 1)
                nc.scalar.activation(ex[:], ex[:], ACT.Exp).then_inc(s_ex, 1)

            @block.vector
            def _(dve):
                n = 0

                def then(ins, sem=None):
                    nonlocal n
                    n += 1
                    ins.then_inc(v, 1)
                    dve.wait_ge(v, n)

                dve.wait_ge(s_high, 1)
                nc.vector.tensor_tensor(wr[1][:], w_router[:], wr[0][:].bitcast(F32), ALU.subtract).then_inc(s_low, 1)
                nc.vector.memset(posm[:], 0.0)
                then(nc.vector.memset(gate[:], 0.0))
                K.W.prepare(dve, "dve", K.W.ahead())
                dve.wait_ge(s_mm, 1)
                then(nc.vector.tensor_copy(lg[:], B[0][:, 0:TT * E].rearrange("p (t e) -> p t e", t=TT)))
                other = lg[:].unsqueeze(2).broadcast_to([P, TT, E, E])
                own = lg[:].unsqueeze(3).broadcast_to([P, TT, E, E])
                before = K.const("before").rearrange("p (e f) -> p e f", e=E).unsqueeze(1).broadcast_to([P, TT, E, E])
                nc.vector.tensor_tensor(ahead[:], other, own, ALU.is_gt)
                then(nc.vector.tensor_tensor(tie[:], other, own, ALU.is_equal))
                then(nc.vector.tensor_tensor(tie[:], tie[:], before, ALU.mult))
                then(nc.vector.tensor_tensor(ahead[:], ahead[:], tie[:], ALU.add))
                then(nc.vector.reduce_sum(rank[:], ahead[:], AX))
                nc.vector.tensor_scalar(ch[:], rank[:], 1.5, None, ALU.is_lt).then_inc(s_ch, 1)
                then(nc.vector.reduce_max(st[:, 0, :], lg[:], AX))
                nc.vector.tensor_tensor(ex[:], lg[:], st[:, 0, :].unsqueeze(2).broadcast_to([P, TT, E]), ALU.subtract).then_inc(s_d, 1)
                dve.wait_ge(s_ex, 1)
                dve.wait_ge(s_ch, 1)
                then(nc.vector.tensor_tensor(ex[:], ex[:], ch[:], ALU.mult))
                then(nc.vector.reduce_sum(st[:, 1, :], ex[:], AX))
                then(nc.vector.reciprocal(st[:, 2, :], st[:, 1, :]))
                nc.vector.tensor_tensor(gate[:, :, 0:E], ex[:], st[:, 2, :].unsqueeze(2).broadcast_to([P, TT, E]), ALU.mult)
                dve.wait_ge(s_mm, 2)
                nc.vector.tensor_tensor(posm[:, :, 0:E], B[1][:, 0:TT * E].rearrange("p (t e) -> p t e", t=TT), ch[:], ALU.mult)
                then(nc.vector.tensor_scalar(ct[:, 0, :], B[2][0:1, 0:E], float(K.cap), None, ALU.is_gt))
                then(nc.vector.memset(ct[:, 1, :], 1.0))
                then(nc.vector.tensor_tensor_scan(ct[:, 2, :], ct[:, 1, :], ct[:, 0, :], 0.0, ALU.mult, ALU.add))
                then(nc.vector.tensor_tensor(ct[:, 3, :], ct[:, 2, :], ct[:, 0, :], ALU.subtract))
                nc.vector.tensor_copy(table[:, 0:E], ct[:, 0, :])
                nc.vector.tensor_copy(table[:, E:2 * E], ct[:, 3, :])
                then(nc.vector.tensor_copy(table[:, 2 * E:], ct[:, 2, E - 1:E]))


def final_norm(K, name):
    nc = K.nc
    with nc.sbuf_tensor("row_" + name, [P, D], F32) as row, nc.Block() as block:
        @block.sync
        def _(sync):
            sync.dma_start(row[:], K.I[name].partition_broadcast(P)).then_inc(K.row_in.sem, 16)
            K.W.issue(sync, K.W.cursor["dve"])

        @block.scalar
        def _(act):
            square_sums(K, nc.scalar)
            act.wait_ge(K.var.sem, K.var.at(1))
            nc.scalar.activation(K.stat[:, 2, :], K.stat[:, 1, :], ACT.Sqrt).then_inc(K.std.sem, 1)

        @block.vector
        def _(dve):
            square_sums(K, nc.vector)
            dve.wait_ge(K.sumsq.sem, K.sumsq.at(TT))
            nc.vector.tensor_scalar(K.stat[:, 1, :], K.stat[:, 0, :], 1.0 / D, EPS, ALU.mult, ALU.add).then_inc(K.var.sem, 1)
            dve.wait_ge(K.std.sem, K.std.at(1))
            nc.vector.reciprocal(K.stat[:, 3, :], K.stat[:, 2, :]).then_inc(K.rstd.sem, 1)
            dve.wait_ge(K.rstd.sem, K.rstd.at(1))
            dve.wait_ge(K.row_in.sem, K.row_in.at(16))
            for t in range(TT):
                nc.vector.scalar_tensor_tensor(out=K.h[:, t, :], in0=K.h[:, t, :], scalar=K.stat[:, 3, t:t + 1], in1=row[:],
                                               op0=ALU.mult, op1=ALU.mult).then_inc(K.scaled.sem, 1)
    for s, n in ((K.sumsq, TT), (K.var, 1), (K.std, 1), (K.rstd, 1), (K.scaled, TT), (K.row_in, 16)):
        s.close(n)


QA, KA, VA, ZA, QB, KB, VB, ZB, GA, GB = range(10)
BEFORE_A, BESIDE_A, BESIDE_B = (QA, KA, VA), (QB, KB, ZA, VB, ZB), (GA, GB)


def plan_hybrid(K, layer):
    w_in = K.I["w_in_2"][layer]
    K.t_before_a, K.t_beside_a, K.t_beside_b = (
        plan_proj(K, w_in, [s * D + half for s in sections for half in (0, 512)], K.slots) for sections in (BEFORE_A, BESIDE_A, BESIDE_B))
    K.t_last = len(K.W.tiles)
    for proj in ("w_proj_a_2", "w_proj_b_2"):
        plan_proj(K, K.I[proj][layer], [0, 512], K.slots)
    out = K.I["w_out_2"][layer].rearrange("(k p) n -> p k n", p=P)
    for k0 in (0, 4):
        for c in (0, 512):
            K.W.plan(K.slots, proj_parts(out, k0, c))


class Beside:

    def __init__(self, K, blocks, dst, banks, lhs=None):
        self.K, self.first, self.n, self.dst, self.banks = K, K.W.taken, len(blocks), dst, banks
        self.lhs = lhs or [K.xT] * self.n
        assert blocks[0] == self.first
        K.W.taken += 2 * self.n

    def pe(self, pe, v):
        K, W, j, half = self.K, self.K.W, v // 2, v % 2
        pe.wait_ge(W.split, self.first + v + 1)
        for t, evac in enumerate((K.evac_act, K.evac_dve)):
            if j and half == 0:
                pe.wait_ge(evac.sem, evac.at(j))
            last = block_half(K.nc, self.banks[t], self.lhs[j], W, (self.first + v) % SPLIT, t, half)
            if t == 1:
                last.then_inc(W.used, 1)
            elif half == 1:
                last.then_inc(K.mm.sem, 1)

    def act(self, act, v):
        K, j = self.K, v // 2
        if v % 2:
            act.wait_ge(K.mm.sem, K.mm.at(j + 1))
            K.nc.scalar.activation(self.dst(j, 0), self.banks[0][:], ACT.Copy).then_inc(K.evac_act.sem, 1)
        K.W.prepare(act, "act", self.first + v + 1 + SPLIT)

    def dve(self, dve, v):
        K, j = self.K, v // 2
        if v % 2:
            dve.wait_ge(K.W.used, self.first + v + 1)
            K.nc.vector.tensor_copy(self.dst(j, 1), self.banks[1][:]).then_inc(K.evac_dve.sem, 1)
        K.W.prepare(dve, "dve", self.first + v + 1 + SPLIT)

    def close(self):
        for sem in (self.K.mm, self.K.evac_act, self.K.evac_dve):
            sem.close(self.n)


def rope(nc, vec, chain, x, cos, sin, tmp):
    a, b = x[:, :, :, 0:8], x[:, :, :, 8:16]
    c, s = (r.rearrange("p (t j) -> p t j", t=TT).unsqueeze(2).broadcast_to([P, TT, A_H, 8]) for r in (cos, sin))
    ac, bs, as_, bc = (tmp[:, 256 * i:256 * (i + 1)].rearrange("p (t h j) -> p t h j", t=TT, h=A_H) for i in range(4))
    vec.tensor_tensor(ac, a, c, ALU.mult)
    vec.tensor_tensor(bs, b, s, ALU.mult)
    vec.tensor_tensor(as_, a, s, ALU.mult)
    chain(vec.tensor_tensor(bc, b, c, ALU.mult))
    vec.tensor_tensor(a, ac, bs, ALU.subtract)
    chain(vec.tensor_tensor(b, as_, bc, ALU.add))


def hybrid(K, layer):
    nc, B, W = K.nc, K.bank, K.W
    if layer:
        lam_init = 0.8 - 0.6 * 2.718281828459045 ** (-0.3 * layer)
    else:
        lam_init = 0.8 - 0.6
    W3 = 3 * P
    norm_transpose(K, [(G_HY0 + KC * layer, K.xT)])
    with ExitStack() as ctx:
        attention = ctx.enter_context(ExitStack())

        def sb(name, shape, dt=F32, ctx=attention):
            return ctx.enter_context(nc.sbuf_tensor(f"hy{layer}_{name}", shape, dt))

        U = sb("u", [P, TT, 8 * D], ctx=ctx)
        lam = sb("lam", [P, 8], ctx=ctx)
        hs = sb("headstat", [P, 4, TT * B_H], ctx=ctx)
        kT, qT = sb("kT", [P, KC, S]), sb("qT", [P, KC, S])
        sc = sb("sc", [P, 2, 2, W3])
        pc = sb("pc", [P, 2, W3])
        pT = sb("pT", [P, 2, W3])
        rope_tmp = sb("rope_tmp", [P, 1024])
        nm = sb("negmax", [P, 2, 2, 2])
        den = sb("den", [P, TT, A_H])
        den2 = sb("den2", [P, 2, 2, 2])
        rden = sb("rden", [P, TT, A_H])
        scale2 = sb("scale2", [P, 2, 2, 2])
        lam_in = sb("lam_in", [P, 4, B_HD])
        sec = lambda i: U[:, :, i * D:(i + 1) * D]
        E = K.hy

        def chunks_a(x):
            return lambda n, c: x[:, c:c + n, :].rearrange("p c s -> p (c s)")

        def chunks_b(x):
            return lambda n, c: x[:, c // 4, (c % 4) * S:(c % 4 + n) * S]

        a_q, a_k, b_q, b_k = chunks_a(qT), chunks_a(kT), chunks_b(sec(QA)), chunks_b(sec(KA))

        def section(sections, where=lambda s: s):
            return lambda j, t: sec(where(sections[j // 2]))[:, t, 512 * (j % 2):512 * (j % 2 + 1)]

        def wait(eng, name, n):
            eng.wait_ge(E[name].sem, E[name].at(n))

        def close(**counts):
            for name, n in counts.items():
                E[name].close(n)

        def turn_pair(q, k, g, banks):
            for src, b in ((sec(q), banks[0]), (sec(k), banks[1])):
                transposes(nc, K, B[b], [src[:, t, c * P:(c + 1) * P] for c in (2 * g, 2 * g + 1) for t in range(TT)]).then_inc(E["qk_turned"].sem, 1)

        def take_q(act, dst, g, n, bank):
            wait(act, "qk_turned", 2 * n + 1)
            nc.scalar.activation(dst(2, 2 * g), B[bank][:], ACT.Copy).then_inc(E["q_out"].sem, 1)

        def take_k(dve, dst, g, n, bank):
            wait(dve, "qk_turned", 2 * n + 2)
            nc.vector.tensor_copy(dst(2, 2 * g), B[bank][:]).then_inc(E["k_out"].sem, 1)

        def scores(bank, q, k, c, row):
            q, k = q(1, c)[row:row + 64, :], k(1, c)[row:row + 64, :]
            nc.tensor.matmul(bank[:, 0:P], q[:, 0:P], k[:, 0:P], start=True, stop=True)
            return nc.tensor.matmul(bank[:, P:W3], q[:, P:S], k, start=True, stop=True)

        PARTS = ((0, slice(0, P)), (1, slice(P, W3)))

        project(K, K.t_before_a, K.xT, section(BEFORE_A))

        beside = Beside(K, K.t_beside_a, section(BESIDE_A), (B[6], B[7]))
        PAIR_AT = {-1: 0, 2: 1, 5: 2, 8: 3}
        PAIR_B_AT = {14: 0, 15: 1, 16: 2, 17: 3}
        LAM_AT, SILU_AT, FIRST_OUT_AT = 6, 12, 13
        NP = len(PAIR_AT)
        STEPS_A = A_H + 4
        assert STEPS_A == 2 * beside.n
        with nc.Block() as block:
            @block.sync
            def _(sync):
                for i, n in enumerate(("lambda_q1_2", "lambda_k1_2", "lambda_q2_2", "lambda_k2_2")):
                    sync.dma_start(lam_in[:, i, :], K.I[n][layer:layer + 1, :].partition_broadcast(P)).then_inc(K.row_in.sem, 16)
                W.issue(sync)

            @block.tensor
            def _(pe):
                def score(h):
                    if h % 4 == 0:
                        wait(pe, "q_out", h // 4 + 1)
                        wait(pe, "k_out", h // 4 + 1)
                    if h:
                        wait(pe, "masked", 2 * h)
                    scores(B[0], a_q, a_k, h // 2, 64 * (h % 2)).then_inc(E["score"].sem, 1)

                def turn(h):
                    wait(pe, "weights", h + 1)
                    if h:
                        wait(pe, "pT", h)
                    transposes(nc, K, B[1], [pc[:, h % 2, i * P:(i + 1) * P] for i in range(3)]).then_inc(E["turned"].sem, 1)

                def values(h):
                    wait(pe, "pT", h + 1)
                    if h == 8:
                        wait(pe, "q_out", NP)
                        wait(pe, "k_out", NP)
                    bank, cols, v = 2 + 2 * (h // 8), slice((h % 8) * 64, (h % 8 + 1) * 64), sec(VA)[:, :, h * 64:(h + 1) * 64]
                    nc.tensor.matmul(B[bank][:, cols], pT[:, h % 2, 0:P], v[:, 0, :], start=True, stop=True)
                    nc.tensor.matmul(B[bank + 1][:, cols], pT[:, h % 2, P:S], v[:, 0, :], start=True, stop=False)
                    nc.tensor.matmul(B[bank + 1][:, cols], pT[:, h % 2, S:W3], v[:, 1, :], start=False, stop=True).then_inc(E["values"].sem, 1)

                beside.pe(pe, 0)
                for i in range(-1, STEPS_A - 1):
                    if i == -1:
                        wait(pe, "roped", 1)
                    if i in PAIR_AT:
                        g = PAIR_AT[i]
                        if g:
                            wait(pe, "q_out", g)
                            wait(pe, "k_out", g)
                        turn_pair(QA, KA, g, (4, 5))
                    if 0 <= i < A_H:
                        score(i)
                    if 0 <= i - 2 < A_H:
                        turn(i - 2)
                    if 0 <= i - 3 < A_H:
                        values(i - 3)
                    if i in PAIR_B_AT:
                        g = PAIR_B_AT[i]
                        if g == 0:
                            wait(pe, "roped_b", 1)
                            wait(pe, "first_out", 1)
                        else:
                            wait(pe, "q_out", NP + g)
                            wait(pe, "k_out", NP + g)
                        turn_pair(QB, KB, g, (2, 3))
                    if i >= 0:
                        beside.pe(pe, i + 1)

            @block.scalar
            def _(act):
                def exp(h):
                    for t, cols in PARTS:
                        wait(act, "masked", 2 * h + t + 1)
                        nc.scalar.activation(sc[:, h % 2, 0, cols], sc[:, h % 2, 0, cols], ACT.Exp, bias=nm[:, h % 2, 0, t:t + 1],
                                             scale=-1.0).then_inc(E["exp"].sem, 1)

                def out(h):
                    wait(act, "turned", h + 1)
                    if h >= 2:
                        wait(act, "values", h - 1)
                    nc.scalar.activation(pT[:, h % 2, :], B[1][:, 0:W3], ACT.Copy).then_inc(E["pT"].sem, 1)

                for i in range(-1, STEPS_A - 1):
                    if i in PAIR_AT:
                        take_q(act, a_q, PAIR_AT[i], PAIR_AT[i], 4)
                    if 0 <= i < A_H:
                        exp(i)
                    if 0 <= i - 2 < A_H:
                        out(i - 2)
                    if i in PAIR_B_AT:
                        take_q(act, b_q, PAIR_B_AT[i], NP + PAIR_B_AT[i], 2)
                    if i == SILU_AT:
                        n = 2 * (BESIDE_A.index(ZA) + 1)
                        act.wait_ge(K.evac_act.sem, K.evac_act.at(n))
                        act.wait_ge(K.evac_dve.sem, K.evac_dve.at(n))
                        nc.scalar.activation(sec(ZA), sec(ZA), ACT.Silu).then_inc(E["silu"].sem, 1)
                    if i == LAM_AT:
                        wait(act, "lam_dot", 2)
                        nc.scalar.activation(lam[:, 2:4], lam[:, 0:2], ACT.Exp).then_inc(E["lam_exp"].sem, 1)
                    beside.act(act, i + 1)
            @block.vector
            def _(dve):
                def chain(ins):
                    ins.then_inc(E["chain"].sem, 1)
                    E["chain"].close(1)
                    dve.wait_ge(E["chain"].sem, E["chain"].base)

                def mask(h):
                    wait(dve, "score", h + 1)
                    if h >= 2:
                        wait(dve, "weights", h - 1)
                    for t, cols in PARTS:
                        nc.vector.tensor_tensor_reduce(out=sc[:, h % 2, 0, cols], in0=B[0][:, cols], in1=K.const("dilneg")[:, cols],
                                                       scale=-(A_HD ** -0.5), scalar=3e38, op0=ALU.add, op1=ALU.min,
                                                       accum_out=nm[:, h % 2, 0, t:t + 1]).then_inc(E["masked"].sem, 1)

                def weigh(h):
                    if h >= 2:
                        wait(dve, "turned", h - 1)
                    for t, cols in PARTS:
                        wait(dve, "exp", 2 * h + t + 1)
                        ins = nc.vector.tensor_tensor_reduce(out=pc[:, h % 2, cols], in0=sc[:, h % 2, 0, cols], in1=K.const("dilcount")[:, cols],
                                                             scale=1.0, scalar=0.0, op0=ALU.mult, op1=ALU.add, accum_out=den[:, t, h:h + 1])
                        if t == 0:
                            chain(ins)
                    ins.then_inc(E["weights"].sem, 1)

                def finish(g):
                    wait(dve, "weights", 8 * g + 8)
                    chain(nc.vector.reciprocal(rden[:, :, 8 * g:8 * g + 8], den[:, :, 8 * g:8 * g + 8]))
                    wait(dve, "values", 8 * g + 8)
                    wait(dve, "silu", 1)
                    for t in range(TT):
                        y = K.xn[:, t, 512 * g:512 * (g + 1)]
                        ins = nc.vector.tensor_tensor(y.rearrange("p (h c) -> p h c", c=64), B[2 + 2 * g + t][:].rearrange("p (h c) -> p h c", c=64),
                                                      rden[:, t, 8 * g:8 * g + 8].unsqueeze(2).broadcast_to([P, 8, 64]), ALU.mult)
                        if t == 0:
                            chain(ins)
                        else:
                            ins.then_inc(E["first_out"].sem, 1)
                            wait(dve, "first_out", g + 1)
                        nc.vector.tensor_tensor(y, y, sec(ZA)[:, t, 512 * g:512 * (g + 1)], ALU.mult)

                heads = lambda i: sec(i).rearrange("p t (h c) -> p t h c", c=A_HD)
                tmp = sc[:].rearrange("p a b w -> p (a b w)")
                for i in (QA, KA):
                    rope(nc, nc.vector, chain, heads(i), K.const("cos"), K.const("sin"), tmp)
                dve.sem_inc(E["roped"].sem, 1)
                for i in range(-1, STEPS_A - 1):
                    if i in PAIR_AT:
                        take_k(dve, a_k, PAIR_AT[i], PAIR_AT[i], 5)
                    if 0 <= i < A_H:
                        mask(i)
                    if 0 <= i - 1 < A_H:
                        weigh(i - 1)
                    if i in PAIR_B_AT:
                        take_k(dve, b_k, PAIR_B_AT[i], NP + PAIR_B_AT[i], 3)
                    if i == FIRST_OUT_AT:
                        finish(0)
                    if i == STEPS_A - 2:
                        finish(1)
                    if i == LAM_AT - 1:
                        dve.wait_ge(K.row_in.sem, K.row_in.at(64))
                        for j in range(2):
                            nc.vector.tensor_tensor_reduce(out=lam_in[:, 2 * j, :], in0=lam_in[:, 2 * j, :], in1=lam_in[:, 2 * j + 1, :], scale=1.0,
                                                           scalar=0.0, op0=ALU.mult, op1=ALU.add, accum_out=lam[:, j:j + 1]).then_inc(E["lam_dot"].sem, 1)
                    if i == LAM_AT + 1:
                        wait(dve, "lam_exp", 1)
                        nc.vector.scalar_tensor_tensor(out=lam[:, 4:5], in0=lam[:, 3:4], scalar=-lam_init, in1=lam[:, 2:3],
                                                       op0=ALU.add, op1=ALU.subtract).then_inc(E["lam"].sem, 1)
                    beside.dve(dve, i + 1)

            @block.gpsimd
            def _(pool):
                def chain(ins):
                    ins.then_inc(E["chain_b"].sem, 1)
                    E["chain_b"].close(1)
                    pool.wait_ge(E["chain_b"].sem, E["chain_b"].base)

                heads = lambda i: sec(i).rearrange("p t (h c) -> p t h c", c=B_HD)
                for i in (QB, KB):
                    n = 2 * (BESIDE_A.index(i) + 1)
                    pool.wait_ge(K.evac_act.sem, K.evac_act.at(n))
                    pool.wait_ge(K.evac_dve.sem, K.evac_dve.at(n))
                    rope(nc, nc.gpsimd, chain, heads(i), K.const("cos"), K.const("sin"), rope_tmp)
                pool.sem_inc(E["roped_b"].sem, 1)

        beside.close()
        K.row_in.close(64)
        close(roped=1, roped_b=1, qk_turned=2 * KC, q_out=KC, k_out=KC, score=A_H, masked=2 * A_H, exp=2 * A_H, weights=A_H, turned=A_H,
              pT=A_H, values=A_H, silu=1, first_out=2, lam_dot=2, lam_exp=1, lam=1)

        ob = sec(QB)
        gates = {GA: VA, GB: ZA}
        beside = Beside(K, K.t_beside_b, section(BESIDE_B, gates.get), (B[6], B[7]))
        STEPS_B = B_H + 3
        tile_at = [v * STEPS_B // (2 * beside.n) for v in range(2 * beside.n)]
        with nc.Block() as block:
            @block.sync
            def _(sync):
                W.issue(sync)

            @block.tensor
            def _(pe):
                def score(h):
                    for m in range(2):
                        if h:
                            wait(pe, "masked", 4 * (h - 1) + 2 * m + 2)
                        scores(B[m], b_q, b_k, h, 64 * m).then_inc(E["score"].sem, 1)

                def turn(h):
                    wait(pe, "weights", h + 1)
                    if h:
                        wait(pe, "pT", h)
                    transposes(nc, K, B[2], [pc[:, h % 2, i * P:(i + 1) * P] for i in range(3)]).then_inc(E["turned"].sem, 1)

                def values(h):
                    wait(pe, "pT", h + 1)
                    if h >= 2:
                        wait(pe, "values_out", h - 1)
                    b, v = B[3 + h % 2], sec(VB)[:, :, h * P:(h + 1) * P]
                    nc.tensor.matmul(b[:, 0:P], pT[:, h % 2, 0:P], v[:, 0, :], start=True, stop=True)
                    nc.tensor.matmul(b[:, P:S], pT[:, h % 2, P:S], v[:, 0, :], start=True, stop=False)
                    nc.tensor.matmul(b[:, P:S], pT[:, h % 2, S:W3], v[:, 1, :], start=False, stop=True).then_inc(E["values"].sem, 1)

                for i in range(STEPS_B):
                    if i < B_H:
                        score(i)
                    if 0 <= i - 2 < B_H:
                        turn(i - 2)
                    if 0 <= i - 3 < B_H:
                        values(i - 3)
                    if i in tile_at:
                        beside.pe(pe, tile_at.index(i))

            @block.scalar
            def _(act):
                def exp(h):
                    for m in range(2):
                        for t, cols in PARTS:
                            wait(act, "masked", 4 * h + 2 * m + t + 1)
                            nc.scalar.activation(sc[:, h % 2, m, cols], sc[:, h % 2, m, cols], ACT.Exp, bias=nm[:, h % 2, m, t:t + 1],
                                                 scale=-1.0, accum_out=den2[:, h % 2, m, t:t + 1]).then_inc(E["exp"].sem, 1)

                def out(h):
                    wait(act, "turned", h + 1)
                    if h >= 2:
                        wait(act, "values", h - 1)
                    nc.scalar.activation(pT[:, h % 2, :], B[2][:, 0:W3], ACT.Copy).then_inc(E["pT"].sem, 1)

                def square(h):
                    wait(act, "values_out", h + 1)
                    if h >= 4:
                        wait(act, "squared", 2 * (h - 3))
                    for t in range(TT):
                        nc.scalar.activation(squares[:, 2 * (h % 4) + t, :], ob[:, t, h * P:(h + 1) * P], ACT.Square,
                                             accum_out=hs[:, 0, t * B_H + h:t * B_H + h + 1]).then_inc(E["squared"].sem, 1)

                squares = rope_tmp[:].rearrange("p (n c) -> p n c", c=P)
                for i in range(STEPS_B):
                    if i < B_H:
                        exp(i)
                    if 0 <= i - 2 < B_H:
                        out(i - 2)
                    if 0 <= i - 3 < B_H:
                        square(i - 3)
                    if i in tile_at:
                        beside.act(act, tile_at.index(i))

            @block.vector
            def _(dve):
                def chain(ins):
                    ins.then_inc(E["chain"].sem, 1)
                    E["chain"].close(1)
                    dve.wait_ge(E["chain"].sem, E["chain"].base)

                def mask(h):
                    if h >= 2:
                        wait(dve, "weights", h - 1)
                    for m in range(2):
                        wait(dve, "score", 2 * h + m + 1)
                        for t, cols in PARTS:
                            nc.vector.tensor_tensor_reduce(out=sc[:, h % 2, m, cols], in0=B[m][:, cols], in1=K.const("causal")[:, cols],
                                                           scale=-(B_HD ** -0.5), scalar=3e38, op0=ALU.add, op1=ALU.min,
                                                           accum_out=nm[:, h % 2, m, t:t + 1]).then_inc(E["masked"].sem, 1)

                def combine(h):
                    p = h % 2
                    wait(dve, "exp", 4 * h + 4)
                    chain(nc.vector.reciprocal(scale2[:, p, :, :], den2[:, p, :, :]))
                    chain(nc.vector.tensor_scalar(scale2[:, p, 1, :], scale2[:, p, 1, :], lam[:, 4:5], None, ALU.mult))
                    if h >= 2:
                        wait(dve, "turned", h - 1)
                    for t, cols in PARTS:
                        ins = nc.vector.tensor_scalar(sc[:, p, 1, cols], sc[:, p, 1, cols], scale2[:, p, 1, t:t + 1], None, ALU.mult)
                    chain(ins)
                    for t, cols in PARTS:
                        ins = nc.vector.scalar_tensor_tensor(out=pc[:, p, cols], in0=sc[:, p, 0, cols], scalar=scale2[:, p, 0, t:t + 1],
                                                             in1=sc[:, p, 1, cols], op0=ALU.mult, op1=ALU.add)
                    ins.then_inc(E["weights"].sem, 1)

                def out(h):
                    wait(dve, "values", h + 1)
                    nc.vector.tensor_copy(ob[:, :, h * P:(h + 1) * P], B[3 + h % 2][:, 0:S].rearrange("p (t c) -> p t c", t=TT)).then_inc(E["values_out"].sem, 1)

                for i in range(STEPS_B):
                    if i < B_H:
                        mask(i)
                    if 0 <= i - 3 < B_H:
                        out(i - 3)
                    if 0 <= i - 1 < B_H:
                        combine(i - 1)
                    if i in tile_at:
                        beside.dve(dve, tile_at.index(i))

        beside.close()
        close(score=2 * B_H, masked=4 * B_H, exp=4 * B_H, weights=B_H, turned=B_H, pT=B_H, values=B_H, values_out=B_H, squared=TT * B_H)

        attention.close()
        ya, yb = (tuple(sb(f"{y}_{half}", [P, KC, S], F32R, ctx) for half in ("high", "low")) for y in ("yaT", "ybT"))
        merged, gate_a, gate_b = sec(QA), sec(VA), sec(ZA)
        flat = lambda b: b[:].rearrange("p (k n) -> p k n", k=4)
        cols = lambda x, j: x[:, 4 * (j % 2):4 * (j % 2) + 4, (j // 2) * P:(j // 2 + 1) * P]
        if layer == 0:
            plan_hybrid(K, 1)

        first = W.taken
        tiles = [("pa", 0, 0), ("pa", 0, 1), ("pa", 1, 0), ("pa", 1, 1), ("pb", 0, 0), ("pb", 0, 1), ("pb", 1, 0), ("pb", 1, 1),
                 ("out", 0, 0), ("out", 1, 0), ("out", 0, 1), ("out", 1, 1)]
        number = {u: v for v, u in enumerate(tiles)}
        ends = [u[:2] for u in tiles if u[2] == 1]
        W.taken += len(tiles)
        with nc.Block() as block:
            @block.sync
            def _(sync):
                W.issue(sync)

            @block.tensor
            def _(pe):
                def turn(src, j, bank):
                    t, hf = j // 2, j % 2
                    transposes(nc, K, B[bank], [src[:, t, (4 * hf + c) * P:(4 * hf + c + 1) * P] for c in range(4)]).then_inc(E["turned"].sem, 1)

                def tile(u, lhs):
                    n = first + number[u]
                    pe.wait_ge(W.split, n + 1)
                    for t in range(TT):
                        last = block_half(nc, B[4 + 2 * u[1] + t], lhs, W, n % SPLIT, t, u[2])
                        if t == 1:
                            last.then_inc(W.used, 1)
                        elif u[2] == 1:
                            last.then_inc(K.mm.sem, 1)

                for j in range(4):
                    turn(K.xn, j, j)
                wait(pe, "k_out", 4)
                tile(tiles[0], ya)
                tile(tiles[1], ya)
                for j in range(4):
                    wait(pe, "yb", j // 2 + 1)
                    turn(ob, j, j)
                tile(tiles[2], ya)
                tile(tiles[3], ya)
                wait(pe, "k_out", 8)
                wait(pe, "product", 2)
                tile(tiles[4], yb)
                tile(tiles[5], yb)
                wait(pe, "product", 4)
                tile(tiles[6], yb)
                wait(pe, "merged", 2)
                for t in range(TT):
                    turn(merged, 2 * t, t)
                tile(tiles[7], yb)
                wait(pe, "k_out", 10)
                tile(tiles[8], K.xT)
                wait(pe, "merged", 4)
                for t in range(TT):
                    turn(merged, 2 * t + 1, 2 + t)
                tile(tiles[9], K.xT)
                wait(pe, "k_out", 12)
                tile(tiles[10], K.xT)
                tile(tiles[11], K.xT)

            @block.scalar
            def _(act):
                def high(dst, j, bank, n, **scale):
                    wait(act, "turned", n)
                    nc.scalar.activation(cols(dst[0], j), flat(B[bank]), ACT.Copy, **scale).then_inc(E["q_out"].sem, 1)

                for j in range(4):
                    high(ya, j, j, j + 1)
                wait(act, "head_var", 1)
                nc.scalar.activation(hs[:, 2, :], hs[:, 1, :], ACT.Sqrt).then_inc(E["head_std"].sem, 1)
                nc.scalar.activation(sec(ZB), sec(ZB), ACT.Silu).then_inc(E["silu"].sem, 1)
                for v in range(len(tiles)):
                    W.prepare(act, "act", first + v + 1 + SPLIT)
                    if v < 2:
                        g = (gate_a, gate_b)[v]
                        nc.scalar.activation(g, g, ACT.Sigmoid).then_inc(E["sigmoid"].sem, 1)
                    if v == 1:
                        wait(act, "lam", 1)
                        for j in range(4):
                            high(yb, j, j, j + 5, scale=lam[:, 5:6])
                    if v in (6, 8):
                        n = v // 2 - 3
                        for t in range(TT):
                            high(K.xT, 2 * t + n, 2 * n + t, 9 + 2 * n + t)
                load_sqrt(K)

            @block.vector
            def _(dve):
                def chain(ins):
                    ins.then_inc(E["chain"].sem, 1)
                    E["chain"].close(1)
                    dve.wait_ge(E["chain"].sem, E["chain"].base)

                def low(dst, j, bank, n):
                    wait(dve, "q_out", n)
                    nc.vector.tensor_tensor(cols(dst[1], j), flat(B[bank]), cols(dst[0], j).bitcast(F32), ALU.subtract).then_inc(E["k_out"].sem, 1)

                def product(name, block_, t):
                    if t == 0:
                        dve.wait_ge(K.mm.sem, K.mm.at(ends.index((name, block_)) + 1))
                    else:
                        dve.wait_ge(W.used, first + number[name, block_, 1] + 1)
                    return B[4 + 2 * block_ + t][:]

                nc.vector.tensor_scalar(hs[:, 1, :], hs[:, 0, :], 1.0 / (2 * B_HD), SUB_EPS, ALU.mult, ALU.add).then_inc(E["head_var"].sem, 1)
                nc.vector.tensor_scalar(lam[:, 5:6], K.gains[:, G_SUB + layer:G_SUB + layer + 1], 1.0 - lam_init, None, ALU.mult).then_inc(E["lam"].sem, 1)
                for j in range(4):
                    low(ya, j, j, j + 1)
                wait(dve, "head_std", 1)
                chain(nc.vector.reciprocal(hs[:, 3, :], hs[:, 2, :]))
                wait(dve, "silu", 1)
                for t in range(TT):
                    for h in range(B_H):
                        o, i = slice(h * P, (h + 1) * P), t * B_H + h
                        ins = nc.vector.scalar_tensor_tensor(out=ob[:, t, o], in0=ob[:, t, o], scalar=hs[:, 3, i:i + 1], in1=sec(ZB)[:, t, o],
                                                             op0=ALU.mult, op1=ALU.mult)
                    ins.then_inc(E["yb"].sem, 1)
                for v, (name, n, half) in enumerate(tiles):
                    W.prepare(dve, "dve", first + v + 1 + SPLIT)
                    if half and name == "pa":
                        wait(dve, "sigmoid", 1)
                        for t in range(TT):
                            c = slice(512 * n, 512 * (n + 1))
                            nc.vector.tensor_tensor(merged[:, t, c], gate_a[:, t, c], product(name, n, t), ALU.mult).then_inc(E["product"].sem, 1)
                    if half and name == "pb":
                        wait(dve, "sigmoid", 2)
                        for t in range(TT):
                            c = slice(512 * n, 512 * (n + 1))
                            nc.vector.tensor_tensor(gate_b[:, t, c], gate_b[:, t, c], product(name, n, t), ALU.mult).then_inc(E["product"].sem, 1)
                            wait(dve, "product", 4 + 2 * n + t + 1)
                            nc.vector.tensor_tensor(merged[:, t, c], merged[:, t, c], gate_b[:, t, c], ALU.add).then_inc(E["merged"].sem, 1)
                    if half and name == "out":
                        for t in range(TT):
                            hv = K.h[:, t, 512 * n:512 * (n + 1)]
                            nc.vector.tensor_tensor(hv, product(name, n, t), hv, ALU.add).then_inc(K.evac_dve.sem, 1)
                    if v == 1:
                        wait(dve, "lam", 1)
                        for j in range(4):
                            wait(dve, "q_out", j + 5)
                            nc.vector.scalar_tensor_tensor(out=cols(yb[1], j), in0=flat(B[j]), scalar=lam[:, 5:6],
                                                           in1=cols(yb[0], j).bitcast(F32), op0=ALU.mult, op1=ALU.subtract).then_inc(E["k_out"].sem, 1)
                    if v in (6, 8):
                        n = v // 2 - 3
                        for t in range(TT):
                            low(K.xT, 2 * t + n, 2 * n + t, 9 + 2 * n + t)
        K.mm.close(6)
        K.evac_dve.close(4)
        close(turned=12, q_out=12, k_out=12, silu=1, head_var=1, head_std=1, lam=1, yb=2, sigmoid=2, product=8, merged=4)


INPUTS = ["x", "gla_w_in", "gla_w_gate_up", "gla_w_out", "sb_w_kv", "sb_w_q", "sb_w_out", "ffn_w_gate", "ffn_w_up", "ffn_w_down",
          "moe_w_router", "moe_w_gate", "moe_w_up", "moe_w_down", "final_norm", "w_in_2", "lambda_q1_2", "lambda_k1_2",
          "lambda_q2_2", "lambda_k2_2", "w_proj_a_2", "w_proj_b_2", "w_out_2", "final_norm_w_2"]


def constants():
    import numpy as np

    i = np.arange(P)
    f = lambda x: np.asarray(x, np.float32)
    t, s = i[:, None], i[None, :]
    tab = {"ident": t == s, "glamask": (t <= s) & (t // GLA_C == s // GLA_C), "later": t > s, "ones": np.ones((P, P)),
           "upto": t <= s, "slots": np.broadcast_to(np.arange(1, 2 * P + 1), (P, 2 * P))}
    if CAP < P:
        tab["slots"] = np.broadcast_to(np.concatenate([np.where(i < CAP, i + 1, -1), i + 1 + CAP]), (P, 2 * P))
    tab["sbmask"] = np.concatenate([t < s, np.ones((P, P)), t < s], 1)
    dist = np.concatenate([t - s, t + P - s, t - s], 1)
    tab["causal"] = np.where(dist >= 0, 0.0, NEG)
    count = sum(((dist >= 0) & (dist <= w) & (dist % d == 0)).astype(int) for w, d in ((128, 1), (512, 4), (2048, 16)))
    tab["dilcount"] = count
    tab["dilneg"] = np.where(count > 0, 0.0, NEG)
    inv = np.float32(1.0) / np.float32(500000.0) ** (np.arange(0, 16, 2, dtype=np.float32) / np.float32(16))
    ang = np.arange(S, dtype=np.float32)[:, None] * inv[None, :]
    lay = lambda a: a.reshape(TT, P, 8).transpose(1, 0, 2).reshape(P, 16)
    tab["cos"], tab["sin"] = lay(np.cos(ang)), lay(np.sin(ang))
    e = np.arange(8)
    tab["before"] = np.broadcast_to((e[None, :] < e[:, None]).reshape(1, 64), (P, 64))
    consts = np.ascontiguousarray(np.concatenate([f(tab[n]) for n, _ in _CONST], 1))
    reset = f(np.arange(GLA_H * S) % GLA_C != 0).reshape(1, -1)
    return consts, reset


def kernel(**inputs):
    import numpy as np
    import concourse.bacc as bacc
    from concourse.bass_utils import run_bass_kernel_spmd as run

    nc = bacc.Bacc("TRN2", target_bir_lowering=False, num_devices=1)
    arrays = {n: np.ascontiguousarray(inputs[n]) for n in INPUTS}
    for n in ("final_norm", "final_norm_w_2"):
        arrays[n] = arrays[n].reshape(1, D)
    chunks = lambda a: np.asarray(a).reshape(-1, P).T
    arrays["gains"] = np.ascontiguousarray(np.concatenate([chunks(a) for a in (
        inputs["attn_norm"][0], inputs["ffn_norm"][0], inputs["kv_norm"], inputs["attn_norm"][1], inputs["ffn_norm"][1],
        inputs["norm_w_2"][0], inputs["norm_w_2"][1], inputs["gla_b_gate"][0], inputs["gla_head_norm"][0],
        inputs["subln_w_2"][0], inputs["subln_w_2"][1])], 1))
    arrays["consts"], arrays["reset"] = constants()
    aps = {n: nc.dram_tensor("in_" + n, a.shape, F32, kind="ExternalInput").ap() for n, a in arrays.items()}
    out = nc.dram_tensor("out", (1, S, D), F32, kind="ExternalOutput").ap()
    build(nc, aps, out, stop=STOP, cap=CAP)
    r = run(nc, [{"in_" + n: a for n, a in arrays.items()}], core_ids=[0])
    return r.results[0]["out"]


STOP = None
```
